# Optimizing a Trainium2 kernel written in Bass

```python
import jax, jax.numpy as jnp
from jax import lax
import numpy as np

D_MODEL = 2048
BATCH = 1
SEQ = 256
DEPTH = 1

D_MIX = D_MODEL
POOL_WIDTH = D_MIX // 4
POOL_WINDOWS = (2, 4, 8, 16)
POOL_GROUPS = len(POOL_WINDOWS)
POOL_GROUP_DIM = POOL_WIDTH // POOL_GROUPS
CONV_WIDTH = D_MIX // 4
CONV_HEADS = 4
CONV_K = 3
NSA_WIDTH = D_MIX - POOL_WIDTH - CONV_WIDTH
HEAD_DIM = 128
NSA_HEADS = NSA_WIDTH // HEAD_DIM
NSA_KV_HEADS = 2
NSA_GROUP = NSA_HEADS // NSA_KV_HEADS
KV_DIM = NSA_KV_HEADS * HEAD_DIM
N_BRANCH = 3
CMP_LEN = 32
CMP_STRIDE = 16
CMP_HIDDEN = 256
SEL_LEN = 64
N_SELECT = 16
SEL_FORCE = 1.0e4
WINDOW = 512
WIN_Q_BLOCK = 128
SEL_Q_BLOCK = 32
D_IN = POOL_WIDTH + 3 * CONV_WIDTH + NSA_WIDTH + 6 * KV_DIM + N_BRANCH * NSA_HEADS
N_GROUPS_MOE = 4
EXPERTS_PER_GROUP = 8
N_EXPERTS = N_GROUPS_MOE * EXPERTS_PER_GROUP
D_EXPERT = 256
TOP_K_EXPERTS = 2
EPS = 1e-6
NEG = -1e30

kernel_name = 'hybrid_pool_conv_nsa_hmoe'

def rmsnorm(x, w):
    xf = x.astype(jnp.float32)
    y = xf * lax.rsqrt(jnp.mean(xf * xf, axis=-1, keepdims=True) + EPS)
    return (y * w.astype(jnp.float32)).astype(x.dtype)

def pool_mixer(u, pool_w, pool_scale):
    B_, S, _ = u.shape
    ug = u.reshape(B_, S, POOL_GROUPS, POOL_GROUP_DIM).astype(jnp.float32)
    cs = jnp.cumsum(ug, axis=1)
    t = jnp.arange(S)
    outs = []
    for g, w in enumerate(POOL_WINDOWS):
        prev = jnp.pad(cs[:, :, g], ((0, 0), (w, 0), (0, 0)))[:, :S]
        cnt = jnp.minimum(t + 1, w).astype(jnp.float32)[None, :, None]
        outs.append((cs[:, :, g] - prev) / cnt)
    pooled = jnp.stack(outs, axis=2)
    mixed = (pooled - ug).astype(u.dtype)
    y = jnp.einsum('bsgc,gcd->bsgd', mixed, pool_w).reshape(B_, S, POOL_WIDTH)
    return y * pool_scale

def conv_mixer(b, c, v, conv_w):
    S = v.shape[1]
    u = c * v
    up = jnp.pad(u, ((0, 0), (CONV_K - 1, 0), (0, 0)))
    y = conv_w[0] * up[:, 0:S]
    for k in range(1, CONV_K):
        y = y + conv_w[k] * up[:, k:k + S]
    return b * y

def compress(kv, pe, w1, w2):
    S = kv.shape[1]
    n_c = (S - CMP_LEN) // CMP_STRIDE + 1
    idx = np.arange(n_c)[:, None] * CMP_STRIDE + np.arange(CMP_LEN)[None, :]
    blk = kv[:, idx] + pe[None, None, :, None, :]
    h = jax.nn.silu(jnp.einsum('bnlhd,lde->bnhe', blk, w1))
    return jnp.einsum('bnhe,ed->bnhd', h, w2)

def nsa_mixer(zc, q_norm_w, k_norm_w, pe_k, w1_k, w2_k, pe_v, w1_v, w2_v):
    B_, S, _ = zc.shape
    Hkv, G, dk = NSA_KV_HEADS, NSA_GROUP, HEAD_DIM
    offs = np.cumsum([0, NSA_WIDTH] + [KV_DIM] * 6)
    q = zc[..., :NSA_WIDTH].reshape(B_, S, Hkv, G, dk)
    q = rmsnorm(q, q_norm_w) * (dk ** -0.5)
    kvs = [zc[..., offs[i + 1]:offs[i + 2]].reshape(B_, S, Hkv, dk) for i in range(6)]
    k_c_raw, v_c_raw, k_s, v_s, k_w, v_w = kvs
    gates = jax.nn.sigmoid(zc[..., offs[-1]:].astype(jnp.float32))
    gates = gates.reshape(B_, S, N_BRANCH, Hkv, G).astype(zc.dtype)
    t = jnp.arange(S)

    k_c = rmsnorm(compress(k_c_raw, pe_k, w1_k, w2_k), k_norm_w[0])
    v_c = compress(v_c_raw, pe_v, w1_v, w2_v)
    n_c = k_c.shape[1]
    cmp_end = jnp.arange(n_c) * CMP_STRIDE + CMP_LEN - 1
    cmask = cmp_end[None, :] <= t[:, None]
    s = jnp.einsum('bshgd,bnhd->bhgsn', q, k_c).astype(jnp.float32)
    p_cmp = jax.nn.softmax(jnp.where(cmask, s, NEG), axis=-1) * cmask
    o_cmp = jnp.einsum('bhgsn,bnhd->bshgd', p_cmp.astype(v_c.dtype), v_c)

    n_sel = S // SEL_LEN
    n_top = min(N_SELECT, n_sel)
    ci = np.arange(n_c)[:, None] * CMP_STRIDE
    sj = np.arange(n_sel)[None, :] * SEL_LEN
    overlap = ((ci < sj + SEL_LEN) & (ci + CMP_LEN > sj)).astype(np.float32)
    imp = jnp.einsum('bhgsn,nj->bhsj', p_cmp, jnp.asarray(overlap))
    blk_ids = jnp.arange(n_sel)
    valid = (blk_ids * SEL_LEN)[None, :] <= t[:, None]
    forced = (blk_ids[None, :] == (t // SEL_LEN)[:, None]) | (blk_ids[None, :] == 0)
    score = jnp.where(forced, SEL_FORCE, jnp.where(valid, imp, -1.0))
    _, sel_idx = lax.top_k(score, n_top)
    k_s = rmsnorm(k_s, k_norm_w[1])
    k_blk = k_s.reshape(B_, n_sel, SEL_LEN, Hkv, dk).transpose(0, 3, 1, 2, 4)
    v_blk = v_s.reshape(B_, n_sel, SEL_LEN, Hkv, dk).transpose(0, 3, 1, 2, 4)
    n_qc = S // SEL_Q_BLOCK
    q_ch = q.reshape(B_, n_qc, SEL_Q_BLOCK, Hkv, G, dk).transpose(1, 0, 3, 4, 2, 5)
    idx_ch = sel_idx.reshape(B_, Hkv, n_qc, SEL_Q_BLOCK, n_top).transpose(2, 0, 1, 3, 4)
    pos_ch = t.reshape(n_qc, SEL_Q_BLOCK)
    bi = jnp.arange(B_)[:, None, None, None]
    hi = jnp.arange(Hkv)[None, :, None, None]

    def sel_block(args):
        qc, ic, pc = args
        kg = k_blk[bi, hi, ic]
        vg = v_blk[bi, hi, ic]
        sc = jnp.einsum('bhgqd,bhqnld->bhgqnl', qc, kg).astype(jnp.float32)
        kpos = ic[..., None] * SEL_LEN + jnp.arange(SEL_LEN)
        m = (kpos <= pc[None, None, :, None, None])[:, :, None]
        sc = jnp.where(m, sc, NEG).reshape(B_, Hkv, G, SEL_Q_BLOCK, n_top * SEL_LEN)
        pr = jax.nn.softmax(sc, axis=-1).reshape(B_, Hkv, G, SEL_Q_BLOCK, n_top, SEL_LEN)
        return jnp.einsum('bhgqnl,bhqnld->bhgqd', pr.astype(vg.dtype), vg)

    o_sel = lax.map(sel_block, (q_ch, idx_ch, pos_ch))
    o_sel = o_sel.transpose(1, 0, 4, 2, 3, 5).reshape(B_, S, Hkv, G, dk)

    k_w = rmsnorm(k_w, k_norm_w[2])
    n_qb = S // WIN_Q_BLOCK
    n_off = WINDOW // WIN_Q_BLOCK + 1

    def band(a):
        ap = jnp.pad(a, ((0, 0), (WINDOW, 0), (0, 0), (0, 0)))
        ap = ap.reshape(B_, n_qb + n_off - 1, WIN_Q_BLOCK, Hkv, dk)
        return jnp.concatenate([ap[:, o:o + n_qb] for o in range(n_off)], axis=2)

    kb, vb = band(k_w), band(v_w)
    qb = q.reshape(B_, n_qb, WIN_Q_BLOCK, Hkv, G, dk)
    sw = jnp.einsum('bnqhgd,bnkhd->bnhgqk', qb, kb).astype(jnp.float32)
    qpos = jnp.arange(n_qb)[:, None] * WIN_Q_BLOCK + jnp.arange(WIN_Q_BLOCK)[None, :]
    kpos = jnp.arange(n_qb)[:, None] * WIN_Q_BLOCK - WINDOW + jnp.arange(n_off * WIN_Q_BLOCK)[None, :]
    d = qpos[:, :, None] - kpos[:, None, :]
    wm = (d >= 0) & (d < WINDOW) & (kpos[:, None, :] >= 0)
    pw = jax.nn.softmax(jnp.where(wm[None, :, None, None], sw, NEG), axis=-1)
    o_win = jnp.einsum('bnhgqk,bnkhd->bnqhgd', pw.astype(vb.dtype), vb).reshape(B_, S, Hkv, G, dk)

    o = (gates[:, :, 0, :, :, None] * o_cmp + gates[:, :, 1, :, :, None] * o_sel
         + gates[:, :, 2, :, :, None] * o_win)
    return o.reshape(B_, S, NSA_WIDTH)

def hier_moe(x, wg, bg, we, be, w_gate, w_up, w_down):
    B_, S, D = x.shape
    xt = x.reshape(B_ * S, D)
    lg = (xt @ wg).astype(jnp.float32) + bg
    grp = jnp.argmax(lg, axis=-1)
    p_grp = jnp.take_along_axis(jax.nn.softmax(lg, axis=-1), grp[:, None], axis=1)
    le = ((xt @ we).astype(jnp.float32) + be).reshape(-1, N_GROUPS_MOE, EXPERTS_PER_GROUP)
    le_g = jnp.take_along_axis(le, grp[:, None, None], axis=1)[:, 0]
    top_p, top_i = lax.top_k(jax.nn.softmax(le_g, axis=-1), TOP_K_EXPERTS)
    w = p_grp * top_p / jnp.sum(top_p, axis=-1, keepdims=True)
    eid = grp[:, None] * EXPERTS_PER_GROUP + top_i
    combine = jnp.sum(jax.nn.one_hot(eid, N_EXPERTS, dtype=jnp.float32) * w[..., None], axis=1)
    h = jax.nn.silu(jnp.einsum('td,edf->tef', xt, w_gate)) * jnp.einsum('td,edf->tef', xt, w_up)
    h = h * combine.astype(h.dtype)[..., None]
    y = jnp.einsum('tef,efd->td', h, w_down)
    return y.reshape(B_, S, D)

def setup_inputs(seed: int = 0) -> dict:
    key = jax.random.key(seed)
    ks = jax.random.split(key, 24)
    L = DEPTH

    def nrm(k, shape, fan_in):
        return jax.random.normal(k, shape, jnp.float32) * (fan_in ** -0.5)

    def gain(k, shape):
        return 1.0 + 0.05 * jax.random.normal(k, shape, jnp.float32)

    return {
        'x': jax.random.normal(ks[0], (BATCH, SEQ, D_MODEL), jnp.float32),
        'norm1_w': gain(ks[1], (L, D_MODEL)),
        'w_in': nrm(ks[2], (L, D_MODEL, D_IN), D_MODEL),
        'pool_w': nrm(ks[3], (L, POOL_GROUPS, POOL_GROUP_DIM, POOL_GROUP_DIM), POOL_GROUP_DIM),
        'pool_scale': gain(ks[4], (L, POOL_WIDTH)),
        'conv_w': nrm(ks[5], (L, CONV_K, CONV_WIDTH), CONV_K),
        'cmp_pe_k': 0.02 * jax.random.normal(ks[6], (L, CMP_LEN, HEAD_DIM), jnp.float32),
        'cmp_w1_k': nrm(ks[7], (L, CMP_LEN, HEAD_DIM, CMP_HIDDEN), CMP_LEN * HEAD_DIM),
        'cmp_w2_k': nrm(ks[8], (L, CMP_HIDDEN, HEAD_DIM), CMP_HIDDEN),
        'cmp_pe_v': 0.02 * jax.random.normal(ks[9], (L, CMP_LEN, HEAD_DIM), jnp.float32),
        'cmp_w1_v': nrm(ks[10], (L, CMP_LEN, HEAD_DIM, CMP_HIDDEN), CMP_LEN * HEAD_DIM),
        'cmp_w2_v': nrm(ks[11], (L, CMP_HIDDEN, HEAD_DIM), CMP_HIDDEN),
        'q_norm_w': gain(ks[12], (L, HEAD_DIM)),
        'k_norm_w': gain(ks[13], (L, N_BRANCH, HEAD_DIM)),
        'w_out': nrm(ks[14], (L, D_MIX, D_MODEL), D_MIX),
        'norm2_w': gain(ks[15], (L, D_MODEL)),
        'router_grp_w': nrm(ks[16], (L, D_MODEL, N_GROUPS_MOE), D_MODEL),
        'router_grp_b': 0.01 * jax.random.normal(ks[17], (L, N_GROUPS_MOE), jnp.float32),
        'router_exp_w': nrm(ks[18], (L, D_MODEL, N_EXPERTS), D_MODEL),
        'router_exp_b': 0.01 * jax.random.normal(ks[19], (L, N_EXPERTS), jnp.float32),
        'exp_w_gate': nrm(ks[20], (L, N_EXPERTS, D_MODEL, D_EXPERT), D_MODEL),
        'exp_w_up': nrm(ks[21], (L, N_EXPERTS, D_MODEL, D_EXPERT), D_MODEL),
        'exp_w_down': nrm(ks[22], (L, N_EXPERTS, D_EXPERT, D_MODEL), D_EXPERT),
    }

def reference(x, norm1_w, w_in, pool_w, pool_scale, conv_w, cmp_pe_k, cmp_w1_k, cmp_w2_k,
              cmp_pe_v, cmp_w1_v, cmp_w2_v, q_norm_w, k_norm_w, w_out, norm2_w,
              router_grp_w, router_grp_b, router_exp_w, router_exp_b,
              exp_w_gate, exp_w_up, exp_w_down):
    a_end = POOL_WIDTH
    b_end = a_end + 3 * CONV_WIDTH
    for l in range(DEPTH):
        xn = rmsnorm(x, norm1_w[l])
        z = xn @ w_in[l]
        y_a = pool_mixer(z[..., :a_end], pool_w[l], pool_scale[l])
        zb = z[..., a_end:b_end]
        y_b = conv_mixer(zb[..., :CONV_WIDTH], zb[..., CONV_WIDTH:2 * CONV_WIDTH],
                         zb[..., 2 * CONV_WIDTH:], conv_w[l])
        y_c = nsa_mixer(z[..., b_end:], q_norm_w[l], k_norm_w[l], cmp_pe_k[l], cmp_w1_k[l], cmp_w2_k[l],
                        cmp_pe_v[l], cmp_w1_v[l], cmp_w2_v[l])
        mixed = jnp.concatenate([y_a, y_b, y_c], axis=-1)
        x = x + mixed @ w_out[l]
        hn = rmsnorm(x, norm2_w[l])
        x = x + hier_moe(hn, router_grp_w[l], router_grp_b[l], router_exp_w[l], router_exp_b[l],
                         exp_w_gate[l], exp_w_up[l], exp_w_down[l])
    return x


_drawn_inputs = setup_inputs


def setup_inputs(seed=0):
    import zlib

    import numpy as np

    out = dict(_drawn_inputs(seed))
    spreads = {}
    factors = {'cmp_pe_k': 7.327,
     'cmp_pe_v': 8.0,
     'q_norm_w': 4.905,
     'k_norm_w': 5.041,
     'router_grp_b': 8.0,
     'router_exp_b': 8.0}
    for name, (base, spread) in spreads.items():
        noise = np.random.default_rng([zlib.crc32(name.encode()), seed]).standard_normal(out[name].shape)
        drawn = base * np.exp(spread * noise) if base else spread * noise
        out[name] = __import__('jax').numpy.asarray(drawn.astype(out[name].dtype))
    for name, factor in factors.items():
        out[name] = (out[name] * factor).astype(out[name].dtype)
    return out
```

```python
from contextlib import ExitStack

import numpy as np

import concourse.bass as bass
from concourse import mybir

F32 = mybir.dt.float32
F32R = mybir.dt.float32r
I32 = mybir.dt.int32
ACT = mybir.ActivationFunctionType
ALU = mybir.AluOpType
AX = mybir.AxisListType.X

P = 128
S = 256
TT = S // P
D = 2048
KC = D // P
HD = 128
NH, NKV = 8, 2
G4 = NH // NKV
WINDOWS = (2, 4, 8, 16)
CMP_LEN, CMP_STRIDE = 32, 16
NC_ = (S - CMP_LEN) // CMP_STRIDE + 1
CH = 256
NGRP, EPG = 4, 8
NEXP = NGRP * EPG
F = 256
EPS = 1e-6
NEG = -1e30
SCALE = float(HD) ** -0.5

QA, QB, CC, KVS, KVW, CV, PU, KVC, CB = range(9)
BLOCK_COL = {QA: 2048, QB: 2560, CC: 1024, KVS: 3584, KVW: 4096, CV: 1536, PU: 0, KVC: 3072, CB: 512}
GATE_COL = 4608
NGATE = 3 * NH

TILE = 2048
RAW, SPL = 6, 3
N_IN, N_CMP, N_OUT = 36, 8, 16
T_CMP = N_IN
T_OUT = T_CMP + N_CMP
T_MOE = T_OUT + N_OUT
PER_GRP = 6 * EPG
LEAD = SPL

R_PE, R_CONV, R_PSC, R_QN, R_KN, N_ROWS = 0, 64, 76, 80, 81, 84
N_SMALL = 15


def layer_kernel(nc, x, norm1_w, w_in, pool_w, pool_scale, conv_w, cmp_pe_k, cmp_w1_k, cmp_w2_k,
                 cmp_pe_v, cmp_w1_v, cmp_w2_v, q_norm_w, k_norm_w, w_out, norm2_w, router_grp_w,
                 router_grp_b, router_exp_w, router_exp_b, exp_w_gate, exp_w_up, exp_w_down, pool_edge, out):
    ctx = ExitStack()
    with ctx:
        def sem(name):
            return ctx.enter_context(nc.semaphore(name))

        def keep(name, shape, dt=F32):
            return ctx.enter_context(nc.sbuf_tensor(name, shape, dt))

        raw = keep("raw", [P, RAW, TILE])
        w_hi = keep("w_hi", [P, SPL, TILE], F32R)
        w_lo = keep("w_lo", [P, SPL, TILE], F32R)
        x1 = keep("x1", [P, TT, D])
        ident = keep("ident", [P, P])
        causal = keep("causal", [P, P])
        cmask = keep("cmask", [P, 2, TT, NC_])
        upper = keep("upper", [P, P])
        ones = keep("ones", [P, P])
        iota = keep("iota", [P, P])
        zero_r = keep("zero_r", [P, P], F32R)
        edge = keep("edge", [P, 4, 16])
        rows = keep("rows", [N_ROWS, P])
        cols = keep("cols", [P, N_ROWS])
        w2 = keep("w2", [P, 2, 2, HD])
        gates = keep("gates", [P, TT, NGATE])
        rbias = keep("rbias", [P, NGRP + NEXP])
        st = keep("st", [P, 64])
        rgw = keep("rgw", [P, KC, NGRP])
        rew = keep("rew", [P, KC, NEXP])
        flags = keep("flags", [1, 2], I32)

        def phase(*tensors):
            with ExitStack() as es:
                return [es.enter_context(nc.sbuf_tensor(*t)) for t in tensors]

        def region(size, *phases):
            got = [phase(*p) for p in phases]
            ctx.enter_context(nc.sbuf_tensor(f"region{region.n}", [P, size // 4], F32))
            region.n += 1
            return got

        region.n = 0
        ((xT_hi, xT_lo), (blk_hi, blk_lo, prob, pT_sb), (hn, xg_hi, xg_lo)) = region(
            32768,
            [("xT_hi", [P, KC, S], F32R), ("xT_lo", [P, KC, S], F32R)],
            [("blk_hi", [P, 2, CMP_LEN, 2 * NC_], F32R), ("blk_lo", [P, 2, CMP_LEN, 2 * NC_], F32R),
             ("prob", [P, 2, G4, S], F32), ("pT_sb", [P, 2, TT, G4 * P], F32)],
            [("hn", [P, TT, D], F32), ("xg_hi", [P, KC, P], F32R), ("xg_lo", [P, KC, P], F32R)],
        )
        ((xn, norm1b), (kvcT, _, pA, pB, wg_lo, etmp, _, work, wgt, wg_hi), (_, blkf), (mix_hi, mix_lo), (hnT,),
         (yg,)) = region(
            32768,
            [("xn", [P, TT, D], F32), ("norm1b", [P, D], F32)],
            [("kvcT", [P, 4, S], F32), ("pad0", [P, 1024], F32), ("pA", [P, 4, S], F32), ("pB", [P, 4, S], F32),
             ("wg_lo", [P, KC, NGATE], F32R), ("etmp", [P, 4, 16], F32), ("pad1", [P, 2048 - 384 - 64], F32),
             ("work", [P, 4, S], F32), ("wgt", [P, KC, NGATE], F32), ("wg_hi", [P, KC, NGATE], F32R)],
            [("pad2", [P, 2048], F32), ("blkf", [P, 2, CMP_LEN, 2 * NC_], F32)],
            [("mix_hi", [P, KC, S], F32R), ("mix_lo", [P, KC, S], F32R)],
            [("hnT", [P, KC, S], F32)],
            [("yg", [P, D], F32)],
        )
        ((qT,), (norm2b,), (sel, selT, hgate, hval, hT_hi, hT_lo)) = region(
            8192,
            [("qT", [P, NH, S], F32)],
            [("norm2b", [P, D], F32)],
            [("sel", [P, TT, P], F32), ("selT", [P, S], F32), ("hgate", [P, F], F32), ("hval", [P, F], F32),
             ("hT_hi", [P, 2, P], F32R), ("hT_lo", [P, 2, P], F32R)],
        )
        ((kT, vnat, znat, cT, poolw, hs, hsT, vc, kcn, kcT, smx), (rt, rw36)) = region(
            23040,
            [("kT", [P, 2, NKV, S], F32), ("vnat", [P, TT, 2, NKV * HD], F32),
             ("znat", [P, TT, 512], F32), ("cT", [P, 4, S], F32),
             ("poolw", [P, 4, P], F32), ("hs", [2 * NC_, 2, CH], F32), ("hsT", [P, 4, 2 * NC_], F32),
             ("vc", [NC_, NKV, HD], F32), ("kcn", [2 * NC_, HD], F32), ("kcT", [P, 2 * NC_], F32),
             ("smx", [P, 3, 12, G4], F32)],
            [("rt", [P, 640], F32), ("rw36", [P, KC, NGRP + NEXP], F32)],
        )
        pT = cT
        ps = ctx.enter_context(nc.psum_tensor("ps", [P, 8, 512], F32))

        raw_in = [sem(f"raw_in{i}") for i in range(RAW)]
        hi_ready, lo_ready, tile_used = sem("hi_ready"), sem("lo_ready"), sem("tile_used")
        x_in, norm1_in, small_in, norm2_in = sem("x_in"), sem("norm1_in"), sem("small_in"), sem("norm2_in")
        masks_ready = sem("masks_ready")
        pool_step, dve_step, act_step = sem("pool_step"), sem("dve_step"), sem("act_step")
        xsq_ready, xms_ready, xrt_ready, xn_ready = sem("xsq_ready"), sem("xms_ready"), sem("xrt_ready"), sem("xn_ready")
        xpose_done, xhi_ready, xlo_ready = sem("xpose_done"), sem("xhi_ready"), sem("xlo_ready")
        cols_done, cols_ready = sem("cols_done"), sem("cols_ready")
        znat_ready, post_done, zT_used = sem("znat_ready"), sem("post_done"), sem("zT_used")
        sq_ready, ms_ready, rt_ready = sem("sq_ready"), sem("ms_ready"), sem("rt_ready")
        v_kept, cT_ready, pT_ready, kvcT_ready = sem("v_kept"), sem("cT_ready"), sem("pT_ready"), sem("kvcT_ready")
        pooled_ready, pooly_done, poolhi_ready = sem("pooled_ready"), sem("pooly_done"), sem("poolhi_ready")
        convy_ready, convhi_ready = sem("convy_ready"), sem("convhi_ready")
        wghi_ready, wglo_ready, gate_done, gexp_ready = sem("wghi_ready"), sem("wglo_ready"), sem("gate_done"), sem("gexp_ready")
        blkf_ready, blkhi_ready, blklo_ready = sem("blkf_ready"), sem("blkhi_ready"), sem("blklo_ready")
        hs_ready, hsT_done, hsT_ready = sem("hs_ready"), sem("hsT_done"), sem("hsT_ready")
        kcv_done, kcsq_ready, kcms_ready, kcrt_ready = sem("kcv_done"), sem("kcsq_ready"), sem("kcms_ready"), sem("kcrt_ready")
        kcn_ready, kcT_done, kcT_ready, vc_ready = sem("kcn_ready"), sem("kcT_done"), sem("kcT_ready"), sem("vc_ready")
        score_done, max_ready, exp_ready, prob_ready = sem("score_done"), sem("max_ready"), sem("exp_ready"), sem("prob_ready")
        pt_done, pt_ready, pv_done, ohi_ready, olo_ready = sem("pt_done"), sem("pt_ready"), sem("pv_done"), sem("ohi_ready"), sem("olo_ready")
        x1_ready = sem("x1_ready")
        ysq_ready, yms_ready, yrt_ready, hn_ready = sem("ysq_ready"), sem("yms_ready"), sem("yrt_ready"), sem("hn_ready")
        hpose_done, hnTa_ready, hnTv_ready, rw36_ready = sem("hpose_done"), sem("hnTa_ready"), sem("hnTv_ready"), sem("rw36_ready")
        logit_done, lexp_in, lexp_ready = sem("logit_done"), sem("lexp_in"), sem("lexp_ready")
        onehot_ready, rank_done, routed = sem("onehot_ready"), sem("rank_done"), sem("routed")
        grp_cols, sel_ready, selT_done, selT_ready = sem("grp_cols"), sem("sel_ready"), sem("selT_done"), sem("selT_ready")
        gather_done, xghi_ready, xglo_ready = sem("gather_done"), sem("xghi_ready"), sem("xglo_ready")
        silu_ready, h_ready, hT_done = sem("silu_ready"), sem("h_ready"), sem("hT_done")
        hThi_ready, hTlo_ready, yg_ready = sem("hThi_ready"), sem("hTlo_ready"), sem("yg_ready")
        scat_done, scat_added, all_added, stored = sem("scat_done"), sem("scat_added"), sem("all_added"), sem("stored")

        col = lambda k: cols[:, k:k + 1]

        def over(ap, dim, shape):
            return ap.unsqueeze(dim).to_broadcast(shape)

        def tile_views(t, kind):
            if kind == "rows":
                return t.rearrange("p (c n) -> p c n", c=4)
            if kind == "gu":
                return t.rearrange("p (w c n) -> p w c n", w=2, c=4)
            return t.rearrange("p (f n) -> p f n", f=2)

        w_in_v = w_in.rearrange("(p c) n -> p c n", c=KC)
        w1_v = [w.rearrange("l d e -> d l e") for w in (cmp_w1_k, cmp_w1_v)]
        w_out_v = w_out.rearrange("(c p) n -> p c n", p=P)
        gate_v = exp_w_gate.rearrange("e (p c) n -> e p c n", c=KC)
        up_v = exp_w_up.rearrange("e (p c) n -> e p c n", c=KC)
        down_v = exp_w_down.rearrange("e (p f) n -> e p f n", f=2)
        out_v = out.rearrange("(t p) n -> p t n", p=P)

        def first_of(q):
            return T_MOE + PER_GRP * q

        def gu_tiles(n0, e):
            return n0 + (4 if isinstance(e, int) and e == 0 else 6 * e + 2)

        block = ctx.enter_context(nc.Block())

        @block.sync
        def _(sp):
            def slot_free(n):
                sp.wait_ge(lo_ready, n - RAW + 1)

            sp.dma_start(x1[:, :, :], x.rearrange("(t p) n -> p t n", p=P)).then_inc(x_in, 16)
            sp.dma_start(norm1b[:, :], norm1_w.partition_broadcast(P)).then_inc(norm1_in, 16)
            for n in range(T_MOE):
                if n >= RAW:
                    slot_free(n)
                if n < T_CMP:
                    b, q = divmod(n, 4)
                    src = w_in_v[:, 4 * q:4 * q + 4, BLOCK_COL[b]:BLOCK_COL[b] + 512]
                elif n < T_OUT:
                    kv, q = divmod(n - T_CMP, 4)
                    src = w1_v[kv][:, 8 * q:8 * q + 8, :]
                else:
                    b, q = divmod(n - T_OUT, 4)
                    src = w_out_v[:, 4 * q:4 * q + 4, 512 * b:512 * b + 512]
                dst = raw[:, n % RAW, :]
                dst = dst.rearrange("p (l e) -> p l e", l=8) if T_CMP <= n < T_OUT else tile_views(dst, "rows")
                sp.dma_start(dst, src).then_inc(raw_in[n % RAW], 16)
                if n == T_OUT + LEAD + RAW:
                    sp.wait_ge(olo_ready, 4)
                    sp.dma_start(norm2b[:, :], norm2_w.partition_broadcast(P)).then_inc(norm2_in, 16)

            def load_gu(e, n, slot, c):
                slot_free(n)
                dst = tile_views(raw[:, slot, :], "gu")
                sp.dma_start(dst[:, 0], gate_v[e, :, 4 * c:4 * c + 4, :]).then_inc(raw_in[slot], 16)
                sp.dma_start(dst[:, 1], up_v[e, :, 4 * c:4 * c + 4, :]).then_inc(raw_in[slot], 16)

            def load_down(e, n, slot, half):
                slot_free(n)
                dst = tile_views(raw[:, slot, :], "down")
                for f in range(2):
                    sp.dma_start(dst[:, f, :], down_v[e, :, f, 1024 * half:1024 * half + 1024]).then_inc(raw_in[slot], 16)

            def group_loads(q, grp):
                n0 = first_of(q)
                for c in range(4):
                    load_gu(grp * EPG, n0 + c, c, c)
                with sp.Fori(1, EPG) as j:
                    for c in range(4):
                        load_gu(grp * EPG + j, n0 + 6 * j - 2 + c, (4 + c) % RAW, c)
                    for half in range(2):
                        load_down(grp * EPG + j - 1, n0 + 6 * j + 2 + half, 2 + half, half)
                for half in range(2):
                    load_down(grp * EPG + EPG - 1, n0 + PER_GRP - 2 + half, 4 + half, half)

            with sp.Fori(0, NGRP) as q:
                group_loads(q, q)
            sp.wait_ge(routed, 1)
            overflow = sp.value_load(flags[0:1, 0:1], min_val=0, max_val=1)
            full_group = sp.value_load(flags[0:1, 1:2], min_val=0, max_val=NGRP - 1)
            with sp.If(overflow > 0):
                group_loads(NGRP, full_group)
            sp.wait_ge(all_added, 1)
            sp.dma_start(out_v, x1[:, :, :]).then_inc(stored, 16)
            sp.wait_ge(stored, 16)

        @block.gpsimd
        def _(pool):
            steps = [0]

            def step(ins):
                steps[0] += 1
                ins.then_inc(pool_step, 1)
                pool.wait_ge(pool_step, steps[0])

            step(pool.memset(ident[:, :], 0.0))
            step(pool.affine_select(out=ident[:, :], in_=ident[:, :], compare_op=ALU.not_equal, fill=1.0,
                                    base=0, pattern=[[-1, P]], channel_multiplier=1))
            step(pool.memset(ones[:, :], 1.0))
            step(pool.memset(zero_r[:, :].bitcast(F32), 0.0))
            step(pool.memset(causal[:, :], 0.0))
            step(pool.affine_select(out=causal[:, :], in_=causal[:, :], compare_op=ALU.is_ge, fill=NEG,
                                    base=0, pattern=[[-1, P]], channel_multiplier=1))
            step(pool.affine_select(out=upper[:, :], in_=ones[:, :], compare_op=ALU.is_ge, fill=0.0,
                                    base=-1, pattern=[[1, P]], channel_multiplier=-1))
            for k, fill in ((0, NEG), (1, 0.0)):
                step(pool.memset(cmask[:, k, :, :], float(k)))
                step(pool.affine_select(out=cmask[:, k, :, :], in_=cmask[:, k, :, :], compare_op=ALU.is_ge,
                                        fill=fill, base=1 - CMP_LEN, pattern=[[P, TT], [-CMP_STRIDE, NC_]],
                                        channel_multiplier=1))
            pool.iota(iota[:, :], pattern=[[1, P]], base=0, channel_multiplier=0,
                      allow_small_or_imprecise_dtypes=True).then_inc(masks_ready, 1)
            for i, b in enumerate((KVS, KVW)):
                pool.wait_ge(znat_ready, 2 * (b + 1))
                pool.tensor_copy(vnat[:, :, i, :], znat[:, :, 256:512]).then_inc(v_kept, 1)
            pool.wait_ge(small_in, 16 * N_SMALL)
            pool.wait_ge(olo_ready, 4)
            pool.tensor_copy(rw36[:, :, 0:NGRP], rgw[:, :, :]).then_inc(rw36_ready, 1)
            pool.tensor_copy(rw36[:, :, NGRP:], rew[:, :, :]).then_inc(rw36_ready, 1)

        @block.scalar
        def _(act):
            def load(dst, src):
                act.dma_start(dst, src).then_inc(small_in, 16)

            load(rows[R_PE:R_PE + 32, :], cmp_pe_k)
            load(rows[R_PE + 32:R_PE + 64, :], cmp_pe_v)
            load(rows[R_CONV:R_PSC, :], conv_w.rearrange("k (j p) -> (k j) p", p=P))
            load(rows[R_PSC:R_QN, :], pool_scale.rearrange("(g p) -> g p", p=P))
            load(rows[R_QN:R_KN, :], q_norm_w.unsqueeze(0))
            load(rows[R_KN:N_ROWS, :], k_norm_w)
            load(edge[:, :, :], pool_edge.partition_broadcast(P))
            load(w2[:, 0], cmp_w2_k.rearrange("(c p) d -> p c d", p=P))
            load(w2[:, 1], cmp_w2_v.rearrange("(c p) d -> p c d", p=P))
            load(wgt[:, :, :], w_in_v[:, :, GATE_COL:GATE_COL + NGATE])
            load(rgw[:, :, :], router_grp_w.rearrange("(p c) g -> p c g", c=KC))
            load(rew[:, :, :], router_exp_w.rearrange("(p c) g -> p c g", c=KC))
            load(rbias[:, 0:NGRP], router_grp_b.partition_broadcast(P))
            load(rbias[:, NGRP:], router_exp_b.partition_broadcast(P))
            load(poolw[:, :, :], pool_w.rearrange("g c d -> c g d"))

            def hi(n, slot=None, rslot=None, count=None):
                slot = n % SPL if slot is None else slot
                rslot = n % RAW if rslot is None else rslot
                act.wait_ge(raw_in[rslot], 16 * (n // RAW + 1) if count is None else count)
                if count is not None or n >= SPL:
                    act.wait_ge(tile_used, n - SPL + 1)
                act.activation(w_hi[:, slot, :], raw[:, rslot, :], ACT.Copy).then_inc(hi_ready, 1)

            act.wait_ge(x_in, 16)
            act.activation(xn[:, 0, :], x1[:, 0, :], ACT.Square, accum_out=st[:, 0:1]).then_inc(xsq_ready, 1)
            act.wait_ge(xms_ready, 1)
            act.activation(st[:, 4:6], st[:, 2:4], ACT.Sqrt).then_inc(xrt_ready, 1)
            hi(0)
            act.wait_ge(cols_done, 1)
            act.activation(cols[:, :], ps[:, 0, 0:N_ROWS], ACT.Copy).then_inc(cols_ready, 1)
            for i in range(8):
                act.wait_ge(xpose_done, i + 1)
                act.activation(xT_hi[:, 2 * i:2 * i + 2, :],
                               ps[:, 4 + i % 4, :].rearrange("p (c t) -> p c t", c=2), ACT.Copy).then_inc(xhi_ready, 1)
            act.wait_ge(small_in, 16 * N_SMALL)
            act.activation(wg_hi[:, :, :], wgt[:, :, :], ACT.Copy).then_inc(wghi_ready, 1)

            n_norm = [0]

            def z_evac(b):
                z = ps[:, 2 * (b % 3):2 * (b % 3) + 2, :]
                act.wait_ge(tile_used, 4 * b + 4)
                if b in (QA, QB, KVS, KVW):
                    w = 512 if b in (QA, QB) else 256
                    if n_norm[0]:
                        act.wait_ge(ms_ready, n_norm[0])
                    act.activation(work[:, :, :].rearrange("p a b -> p (a b)")[:, 0:2 * w].rearrange("p (t n) -> p t n", t=2),
                                   z[:, :, 0:w], ACT.Square).then_inc(sq_ready, 1)
                    n_norm[0] += 1
                    if w == 256:
                        act.wait_ge(post_done, b)
                        if b == KVW:
                            act.wait_ge(v_kept, 1)
                        act.activation(znat[:, :, 256:512], z[:, :, 256:512], ACT.Copy).then_inc(znat_ready, 1)
                    act.wait_ge(ms_ready, n_norm[0])
                    act.activation(st[:, 16:16 + w // 64], st[:, 8:8 + w // 64], ACT.Sqrt).then_inc(rt_ready, 1)
                    return
                act.wait_ge(post_done, b)
                if b == CV:
                    act.wait_ge(v_kept, 2)
                act.activation(znat[:, 0, :], z[:, 0, :], ACT.Copy).then_inc(znat_ready, 1)

            def zT_evac(b):
                zT = ps[:, 6:8, :].rearrange("p b (h t) -> p (b h) t", h=2)
                if b in (CV, CB):
                    return
                act.wait_ge(post_done, b + 1)
                if b in (QA, QB):
                    act.activation(qT[:, 4 * b:4 * b + 4, :], zT, ACT.Copy, scale=col(R_QN)).then_inc(zT_used, 1)
                elif b == CC:
                    act.activation(cT[:, :, :], zT, ACT.Copy).then_inc(zT_used, 1)
                elif b in (KVS, KVW):
                    k = b - KVS
                    act.activation(kT[:, k, :, :], zT[:, 0:2, :], ACT.Copy, scale=col(R_KN + 1 + k)).then_inc(zT_used, 1)
                elif b == PU:
                    act.activation(pT[:, :, :], zT, ACT.Copy).then_inc(zT_used, 1)
                elif b == KVC:
                    act.activation(kvcT[:, :, :], zT, ACT.Copy).then_inc(zT_used, 1)

            for n in range(1, T_CMP + 2):
                hi(n)
                if n >= 5 and n % 4 == 1:
                    b = (n - 5) // 4
                    z_evac(b)
                    if b % 3 >= 1:
                        zT_evac(b - 1)
                    if b % 3 == 2:
                        zT_evac(b)

            act.wait_ge(blkf_ready, 1)
            act.wait_ge(gate_done, 1)
            act.activation(blk_hi[:, :, :, :], blkf[:, :, :, :], ACT.Copy).then_inc(blkhi_ready, 1)
            act.wait_ge(pooly_done, 1)
            for g in range(4):
                act.activation(mix_hi[:, g, :], ps[:, g // 2, (g % 2) * S:(g % 2) * S + S], ACT.Copy,
                               scale=col(R_PSC + g)).then_inc(poolhi_ready, 1)
            act.wait_ge(convy_ready, 1)
            act.activation(mix_hi[:, 4:8, :], work[:, :, :], ACT.Copy).then_inc(convhi_ready, 1)
            for n in range(T_CMP + 2, T_OUT):
                hi(n)
            for kv in range(2):
                act.wait_ge(tile_used, T_CMP + 4 * kv + 4)
                act.activation(hs[:, kv, :], ps[0:2 * NC_, 4 + kv, 0:CH], ACT.Silu).then_inc(hs_ready, 1)
            act.wait_ge(hsT_done, 1)
            act.activation(hsT[:, :, :], ps[:, 6, 0:128].rearrange("p (k n) -> p k n", k=4)[:, :, 0:2 * NC_],
                           ACT.Copy).then_inc(hsT_ready, 1)
            act.wait_ge(kcv_done, 1)
            act.activation(kcn[:, :], ps[0:2 * NC_, 7, 0:HD], ACT.Square, accum_out=st[0:2 * NC_, 24:25]).then_inc(kcsq_ready, 1)
            act.wait_ge(kcms_ready, 1)
            act.activation(st[0:2 * NC_, 26:27], st[0:2 * NC_, 25:26], ACT.Sqrt).then_inc(kcrt_ready, 1)
            act.wait_ge(kcT_done, 1)
            act.activation(kcT[:, :], ps[:, 6, 256:256 + 2 * NC_], ACT.Copy, scale=col(R_KN)).then_inc(kcT_ready, 1)
            act.wait_ge(gate_done, 1)
            act.activation(gates[:, :, :], ps[:, 2:4, 0:NGATE], ACT.Exp, scale=-1.0).then_inc(gexp_ready, 1)
            for n in range(T_OUT, T_OUT + LEAD):
                hi(n)

            def exps(j):
                tt, kind = (j // 3) % 2, j % 3
                n = NC_ if kind == 2 else P * (tt + 1)
                act.wait_ge(max_ready, j + 1)
                if j >= 2:
                    act.wait_ge(pt_done, j - 1)
                for h in range(G4):
                    s = ps[:, 4, 16 * h:16 * h + n] if kind == 2 else \
                        ps[:, 2 * kind + h // 2, (h % 2) * S:(h % 2) * S + n]
                    act.activation(prob[:, j % 2, h, 0:n], s, ACT.Exp, bias=smx[:, 0, j, h:h + 1],
                                   accum_out=smx[:, 1, j, h:h + 1]).then_inc(exp_ready, 1)

            def pt_evac(j):
                tt, kind = (j // 3) % 2, j % 3
                act.wait_ge(pt_done, j + 1)
                if j >= 2:
                    act.wait_ge(pv_done, j - 1)
                if kind == 2:
                    act.activation(pT_sb[0:NC_, j % 2, 0, :], ps[0:NC_, 5, :], ACT.Copy).then_inc(pt_ready, 1)
                else:
                    act.activation(pT_sb[:, j % 2, 0:tt + 1, :], ps[:, 5:6 + tt, :], ACT.Copy).then_inc(pt_ready, 1)

            def o_hi(u):
                kv, tt = divmod(u, 2)
                act.wait_ge(pv_done, 3 * (u + 1))
                act.activation(mix_hi[:, 8 + G4 * kv:8 + G4 * kv + G4, P * tt:P * tt + P],
                               ps[:, 7, :].rearrange("p (h t) -> p h t", h=G4), ACT.Copy).then_inc(ohi_ready, 1)

            exps(0)
            for j in range(12):
                if j < 11:
                    exps(j + 1)
                if j % 3 == 0 and j:
                    o_hi(j // 3 - 1)
                pt_evac(j)
            o_hi(3)

            for n in range(T_OUT + LEAD, T_MOE + LEAD - 1):
                if n < T_MOE:
                    hi(n)
                else:
                    hi(n, count=160 + 32)

            act.wait_ge(x1_ready, 4)
            hi(T_MOE + LEAD - 1, count=160 + 32)
            act.activation(hn[:, 0, :], x1[:, 0, :], ACT.Square, accum_out=st[:, 32:33]).then_inc(ysq_ready, 1)
            act.wait_ge(yms_ready, 1)
            act.activation(st[:, 36:38], st[:, 34:36], ACT.Sqrt).then_inc(yrt_ready, 1)
            for i in range(0, 8, 2):
                act.wait_ge(hpose_done, i + 1)
                act.activation(hnT[:, 2 * i:2 * i + 2, :],
                               ps[:, 4 + i % 4, :].rearrange("p (c t) -> p c t", c=2), ACT.Copy).then_inc(hnTa_ready, 1)
            act.wait_ge(lexp_in, 1)
            act.activation(rt[:, 80:90], rt[:, 80:90], ACT.Exp).then_inc(lexp_ready, 1)

            def group_work(q):
                n0 = first_of(q)
                uses = 160 + 32 * EPG * q

                def hi_at(n, p, local):
                    hi(n, slot=p % SPL, rslot=p % RAW, count=uses + 32 * (local + 1))

                for r in range(4):
                    act.wait_ge(gather_done, 4 * q + r + 1)
                    act.activation(xg_hi[:, 4 * r:4 * r + 4, :],
                                   ps[:, 5 + r % 2, :].rearrange("p (c t) -> p c t", c=4), ACT.Copy).then_inc(xghi_ready, 1)
                hi_at(n0 + 3, 3, 0)

                def silu(e):
                    act.wait_ge(tile_used, gu_tiles(n0, e))
                    act.activation(hgate[:, :], ps[:, 4, 0:F], ACT.Silu).then_inc(silu_ready, 1)

                def hT_evac(e):
                    act.wait_ge(hT_done, EPG * q + e + 1)
                    act.activation(hT_hi[:, :, :], ps[:, 7, 0:S].rearrange("p (f t) -> p f t", f=2),
                                   ACT.Copy).then_inc(hThi_ready, 1)

                silu(0)
                with act.Fori(1, EPG) as j:
                    base = n0 + 6 * j - 2
                    for c in range(4):
                        hi_at(base + c, 4 + c, j - 1 if c < 2 else j)
                        if c == 1:
                            hT_evac(j - 1)
                    for half in range(2):
                        hi_at(base + 4 + half, 2 + half, j)
                    silu(j)
                for half in range(2):
                    hi_at(n0 + PER_GRP - 2 + half, 4 + half, EPG - 1)
                hT_evac(EPG - 1)
                act.wait_ge(tile_used, n0 + PER_GRP)
                for nb in (0, 2):
                    act.activation(yg[:, 512 * nb:512 * nb + 512], ps[:, nb, :], ACT.Copy).then_inc(yg_ready, 1)

            def group_lead(q):
                for i in range(LEAD):
                    hi(first_of(q) + i, slot=i, rslot=i, count=160 + 32 * EPG * q + 32)

            group_work(0)
            with act.Fori(1, NGRP) as q:
                group_lead(q)
                group_work(q)
            act.wait_ge(routed, 1)
            overflow = act.value_load(flags[0:1, 0:1], min_val=0, max_val=1)
            with act.If(overflow > 0):
                group_lead(NGRP)
                group_work(NGRP)

        @block.vector
        def _(dve):
            steps = [0]

            def step(ins):
                steps[0] += 1
                ins.then_inc(dve_step, 1)
                dve.wait_ge(dve_step, steps[0])

            def lo(n, slot=None, rslot=None):
                slot = n % SPL if slot is None else slot
                rslot = n % RAW if rslot is None else rslot
                dve.wait_ge(hi_ready, n + 1)
                dve.tensor_tensor(w_lo[:, slot, :], raw[:, rslot, :], w_hi[:, slot, :].bitcast(F32),
                                  ALU.subtract).then_inc(lo_ready, 1)

            dve.wait_ge(x_in, 16)
            step(dve.tensor_tensor_reduce(out=xn[:, 1, :], in0=x1[:, 1, :], in1=x1[:, 1, :], scale=1.0, scalar=0.0,
                                          op0=ALU.mult, op1=ALU.add, accum_out=st[:, 1:2]))
            dve.wait_ge(xsq_ready, 1)
            dve.tensor_scalar(st[:, 2:4], st[:, 0:2], 1.0 / D, EPS, ALU.mult, ALU.add).then_inc(xms_ready, 1)
            dve.wait_ge(xrt_ready, 1)
            step(dve.reciprocal(st[:, 6:8], st[:, 4:6]))
            dve.wait_ge(norm1_in, 16)
            for t in range(TT):
                dve.scalar_tensor_tensor(out=xn[:, t, :], in0=x1[:, t, :], scalar=st[:, 6 + t:7 + t], in1=norm1b[:, :],
                                         op0=ALU.mult, op1=ALU.mult).then_inc(xn_ready, 1)
            lo(0)
            for i in range(8):
                dve.wait_ge(xhi_ready, i + 1)
                dve.tensor_tensor(xT_lo[:, 2 * i:2 * i + 2, :], ps[:, 4 + i % 4, :].rearrange("p (c t) -> p c t", c=2),
                                  xT_hi[:, 2 * i:2 * i + 2, :].bitcast(F32), ALU.subtract).then_inc(xlo_ready, 1)
            dve.wait_ge(wghi_ready, 1)
            dve.tensor_tensor(wg_lo[:, :, :], wgt[:, :, :], wg_hi[:, :, :].bitcast(F32), ALU.subtract).then_inc(wglo_ready, 1)
            dve.wait_ge(cols_ready, 1)
            dve.tensor_scalar(col(R_QN), col(R_QN), SCALE, None, ALU.mult).then_inc(zT_used, 1)

            n_norm = [0]

            def z_evac(b):
                z = ps[:, 2 * (b % 3):2 * (b % 3) + 2, :]
                if b in (QA, QB, KVS, KVW):
                    w = 512 if b in (QA, QB) else 256
                    nh = w // HD
                    n_norm[0] += 1
                    dve.wait_ge(sq_ready, n_norm[0])
                    sq = work[:, :, :].rearrange("p a b -> p (a b)")[:, 0:2 * w]
                    step(dve.tensor_reduce(st[:, 48:48 + 2 * nh], sq.rearrange("p (h d) -> p h d", d=HD), AX, ALU.add))
                    dve.tensor_scalar(st[:, 8:8 + 2 * nh], st[:, 48:48 + 2 * nh], 1.0 / HD, EPS, ALU.mult,
                                      ALU.add).then_inc(ms_ready, 1)
                    dve.wait_ge(rt_ready, n_norm[0])
                    step(dve.reciprocal(st[:, 24:24 + 2 * nh], st[:, 16:16 + 2 * nh]))
                    if b:
                        dve.wait_ge(post_done, b)
                    if b == KVW:
                        dve.wait_ge(v_kept, 1)
                    for t in range(TT):
                        r = st[:, 24 + nh * t:24 + nh * t + nh]
                        ins = dve.tensor_tensor(znat[:, t, 0:w].rearrange("p (h d) -> p h d", d=HD),
                                                z[:, t, 0:w].rearrange("p (h d) -> p h d", d=HD),
                                                over(r, 2, [P, nh, HD]), ALU.mult)
                        if w == 512 or t:
                            ins.then_inc(znat_ready, 1)
                    return
                dve.wait_ge(tile_used, 4 * b + 4)
                dve.wait_ge(post_done, b)
                if b == CV:
                    dve.wait_ge(v_kept, 2)
                dve.tensor_copy(znat[:, 1, :], z[:, 1, :]).then_inc(znat_ready, 1)

            zT = ps[:, 6:8, :].rearrange("p b (h t) -> p (b h) t", h=2)

            def after_v():
                dve.wait_ge(post_done, CV + 1)
                dve.wait_ge(zT_used, CC + 2)
                step(dve.tensor_tensor(cT[:, :, :], zT, cT[:, :, :], ALU.mult))
                dve.sem_inc(zT_used, 1)
                for j in range(4):
                    step(dve.tensor_scalar(work[:, j, :], cT[:, j, :], col(R_CONV + 8 + j), None, ALU.mult))
                    for shift, k in ((1, 1), (2, 0)):
                        step(dve.scalar_tensor_tensor(out=work[:, j, shift:], in0=cT[:, j, 0:S - shift],
                                                      scalar=col(R_CONV + 4 * k + j), in1=work[:, j, shift:],
                                                      op0=ALU.mult, op1=ALU.add))

            def after_pool():
                dve.wait_ge(zT_used, PU + 2)
                src, dst = pT, pA
                for level, shift in enumerate((1, 2, 4, 8)):
                    g = slice(level, 4)
                    dve.tensor_copy(dst[:, g, 0:shift], src[:, g, 0:shift])
                    step(dve.tensor_tensor(dst[:, g, shift:], src[:, g, shift:], src[:, g, 0:S - shift], ALU.add))
                    src, dst = dst, (pB if dst is pA else pA)
                for g, w in enumerate(WINDOWS):
                    s = pA if g % 2 == 0 else pB
                    step(dve.tensor_tensor(etmp[:, g, :], s[:, g, 0:16], edge[:, g, :], ALU.mult))
                    step(dve.tensor_tensor(etmp[:, g, :], etmp[:, g, :], pT[:, g, 0:16], ALU.subtract))
                    step(dve.scalar_tensor_tensor(out=pT[:, g, :], in0=s[:, g, :], scalar=1.0 / w, in1=pT[:, g, :],
                                                  op0=ALU.mult, op1=ALU.subtract))
                dve.tensor_copy(pT[:, :, 0:16], etmp[:, :, :]).then_inc(pooled_ready, 1)

            def after_kvc():
                dve.wait_ge(zT_used, KVC + 2)
                for kv in range(2):
                    for lh in range(2):
                        for h in range(NKV):
                            src = kvcT[:, 2 * kv + h, :].rearrange("p (n l) -> p n l", l=CMP_STRIDE)[:, lh:lh + NC_, :]
                            pe = cols[:, R_PE + 32 * kv + 16 * lh:R_PE + 32 * kv + 16 * lh + 16]
                            dst = blkf[:, kv, 16 * lh:16 * lh + 16, NC_ * h:NC_ * h + NC_].rearrange("p l n -> p n l")
                            ins = dve.tensor_tensor(dst, src, over(pe, 1, [P, NC_, CMP_STRIDE]), ALU.add)
                ins.then_inc(blkf_ready, 1)

            for n in range(1, T_CMP + 2):
                lo(n)
                if n >= 5 and n % 4 == 1:
                    b = (n - 5) // 4
                    z_evac(b)
                    if b == CV:
                        after_v()
                    if b == KVC:
                        after_pool()
            after_kvc()
            dve.wait_ge(post_done, CB + 1)
            step(dve.tensor_tensor(work[:, :, :], zT, work[:, :, :], ALU.mult))
            dve.sem_inc(zT_used, 1)
            dve.sem_inc(convy_ready, 1)
            dve.wait_ge(blkhi_ready, 1)
            dve.tensor_tensor(blk_lo[:, :, :, :], blkf[:, :, :, :], blk_hi[:, :, :, :].bitcast(F32),
                              ALU.subtract).then_inc(blklo_ready, 1)
            for g in range(4):
                dve.wait_ge(poolhi_ready, 2 * (g // 2) + 2)
                dve.scalar_tensor_tensor(out=mix_lo[:, g, :], in0=ps[:, g // 2, (g % 2) * S:(g % 2) * S + S],
                                         scalar=col(R_PSC + g), in1=mix_hi[:, g, :].bitcast(F32),
                                         op0=ALU.mult, op1=ALU.subtract)
            dve.wait_ge(convhi_ready, 1)
            step(dve.tensor_tensor(mix_lo[:, 4:8, :], work[:, :, :], mix_hi[:, 4:8, :].bitcast(F32), ALU.subtract))
            for n in range(T_CMP + 2, T_OUT):
                lo(n)
            dve.wait_ge(kcsq_ready, 1)
            dve.tensor_copy(vc[:, :, :], ps[0:NC_, 7, HD:3 * HD].rearrange("p (h d) -> p h d", h=2)).then_inc(vc_ready, 1)
            dve.tensor_scalar(st[0:2 * NC_, 25:26], st[0:2 * NC_, 24:25], 1.0 / HD, EPS, ALU.mult, ALU.add).then_inc(kcms_ready, 1)
            dve.wait_ge(kcrt_ready, 1)
            step(dve.reciprocal(st[0:2 * NC_, 27:28], st[0:2 * NC_, 26:27]))
            dve.tensor_scalar(kcn[:, :], ps[0:2 * NC_, 7, 0:HD], st[0:2 * NC_, 27:28], None, ALU.mult).then_inc(kcn_ready, 1)
            dve.wait_ge(gexp_ready, 1)
            step(dve.tensor_scalar(gates[:, :, :], gates[:, :, :], 1.0, None, ALU.add))
            step(dve.reciprocal(gates[:, :, :], gates[:, :, :]))
            for n in range(T_OUT, T_OUT + LEAD):
                lo(n)

            def score_view(j, n):
                if j % 3 == 2:
                    return ps[:, 4, 0:64].rearrange("p (h n) -> p h n", h=G4)[:, :, 0:n]
                return ps[:, 2 * (j % 3):2 * (j % 3) + 2, :].rearrange("p b (h s) -> p (b h) s", h=2)[:, :, 0:n]

            def mask_max(j):
                tt, kind = (j // 3) % 2, j % 3
                dve.wait_ge(score_done, j + 1)
                if kind == 2:
                    s = score_view(j, NC_)
                    step(dve.tensor_tensor(s, s, over(cmask[:, 0, tt, :], 1, [P, G4, NC_]), ALU.add))
                else:
                    s = score_view(j, P * (tt + 1))
                    d = s[:, :, P * tt:P * tt + P]
                    step(dve.tensor_tensor(d, d, over(causal[:, :], 1, [P, G4, P]), ALU.add))
                dve.tensor_reduce(smx[:, 0, j, :], s, AX, ALU.max, negate=True).then_inc(max_ready, 1)

            def scale_probs(j):
                u, kind = divmod(j, 3)
                kv, tt = divmod(u, 2)
                n = NC_ if kind == 2 else P * (tt + 1)
                dve.wait_ge(exp_ready, 4 * (j + 1))
                step(dve.reciprocal(smx[:, 2, j, :], smx[:, 1, j, :]))
                g0 = NH * (0 if kind == 2 else kind + 1) + G4 * kv
                step(dve.tensor_tensor(smx[:, 2, j, :], smx[:, 2, j, :], gates[:, tt, g0:g0 + G4], ALU.mult))
                p = prob[:, j % 2, :, 0:n]
                ins = dve.tensor_tensor(p, p, over(smx[:, 2, j, :], 2, [P, G4, n]), ALU.mult)
                if kind == 2:
                    step(ins)
                    ins = dve.tensor_tensor(p, p, over(cmask[:, 1, tt, :], 1, [P, G4, NC_]), ALU.mult)
                ins.then_inc(prob_ready, 1)

            def o_lo(u):
                kv, tt = divmod(u, 2)
                dve.wait_ge(ohi_ready, u + 1)
                hs_ = slice(8 + G4 * kv, 8 + G4 * kv + G4)
                dve.tensor_tensor(mix_lo[:, hs_, P * tt:P * tt + P], ps[:, 7, :].rearrange("p (h t) -> p h t", h=G4),
                                  mix_hi[:, hs_, P * tt:P * tt + P].bitcast(F32), ALU.subtract).then_inc(olo_ready, 1)

            mask_max(0)
            for j in range(12):
                if j < 11:
                    mask_max(j + 1)
                scale_probs(j)
                if j % 3 == 0 and j:
                    o_lo(j // 3 - 1)
            o_lo(3)

            for n in range(T_OUT + LEAD, T_MOE + LEAD):
                if n < T_MOE + LEAD - 1:
                    lo(n)
                if (n - T_OUT) % 4 == 1 and n >= T_OUT + 5:
                    b = (n - T_OUT - 5) // 4
                    dve.wait_ge(tile_used, T_OUT + 4 * b + 4)
                    v = x1[:, :, 512 * b:512 * b + 512]
                    dve.tensor_tensor(v, v, ps[:, 2 * (b % 2):2 * (b % 2) + 2, :], ALU.add).then_inc(x1_ready, 1)

            dve.wait_ge(x1_ready, 4)
            step(dve.tensor_tensor_reduce(out=hn[:, 1, :], in0=x1[:, 1, :], in1=x1[:, 1, :], scale=1.0, scalar=0.0,
                                          op0=ALU.mult, op1=ALU.add, accum_out=st[:, 33:34]))
            dve.wait_ge(ysq_ready, 1)
            dve.tensor_scalar(st[:, 34:36], st[:, 32:34], 1.0 / D, EPS, ALU.mult, ALU.add).then_inc(yms_ready, 1)
            dve.wait_ge(yrt_ready, 1)
            step(dve.reciprocal(st[:, 38:40], st[:, 36:38]))
            dve.wait_ge(norm2_in, 16)
            for t in range(TT):
                dve.scalar_tensor_tensor(out=hn[:, t, :], in0=x1[:, t, :], scalar=st[:, 38 + t:39 + t], in1=norm2b[:, :],
                                         op0=ALU.mult, op1=ALU.mult).then_inc(hn_ready, 1)
            lo(T_MOE + LEAD - 1)
            for i in range(1, 8, 2):
                dve.wait_ge(hpose_done, i + 1)
                dve.tensor_copy(hnT[:, 2 * i:2 * i + 2, :],
                                ps[:, 4 + i % 4, :].rearrange("p (c t) -> p c t", c=2)).then_inc(hnTv_ready, 1)

            def rv(a, *dims):
                n = TT * int(np.prod(dims))
                v = rt[:, a:a + n]
                if len(dims) == 2:
                    return v.rearrange("p (t a b) -> p t a b", t=TT, a=dims[0])
                return v.rearrange("p (t a) -> p t a", t=TT)

            L = rv(0, 36)
            gmax, lexp = rv(72, 1), rv(80, 4)
            diff = rv(88, 1)
            tie, pg = rv(92, 4), rv(100, 1)
            prod, leg, leg2 = rv(104, 4, 8), rv(168, 8), rv(184, 8)
            m1, m2, E, O1, O2 = rv(200, 1), rv(202, 1), rv(204, 8), rv(220, 8), rv(236, 8)
            wa, wb = rv(252, 1), rv(254, 1)
            cmb = rv(256, 8)
            Gm, rank = rv(272, 5), rv(282, 5)
            cnt_over, tmp4, ov = rt[:, 292:296], rv(296, 4), rt[:, 304:306]
            tied, order8, order4 = rv(306, 1), rt[:, 320:328], rt[:, 328:332]
            tmp8 = rv(332, 8)

            step(dve.tensor_scalar(order8, iota[:, 0:8], -1.0, 8.0, ALU.mult, ALU.add))
            step(dve.tensor_scalar(order4, iota[:, 0:4], -1.0, 4.0, ALU.mult, ALU.add))
            dve.wait_ge(logit_done, 1)
            step(dve.tensor_tensor(L, ps[:, 0:2, 0:36], over(rbias[:, :], 1, [P, TT, 36]), ALU.add))
            lg = L[:, :, 0:4]
            le = L[:, :, 4:36].rearrange("p t (g e) -> p t g e", g=NGRP)

            def argmax_first(one_hot, values, order, n, top):
                step(dve.tensor_reduce(top, values, AX, ALU.max))
                step(dve.tensor_tensor(E[:, :, 0:n], values, top.to_broadcast([P, TT, n]), ALU.is_equal))
                step(dve.tensor_tensor(E[:, :, 0:n], E[:, :, 0:n], over(order, 1, [P, TT, n]), ALU.mult))
                step(dve.tensor_reduce(tied, E[:, :, 0:n], AX, ALU.max))
                step(dve.tensor_tensor(one_hot, E[:, :, 0:n], tied.to_broadcast([P, TT, n]), ALU.is_equal))

            argmax_first(Gm[:, :, 0:4], lg, order4, 4, gmax)
            dve.sem_inc(onehot_ready, 1)
            step(dve.tensor_tensor(lexp, lg, gmax.to_broadcast([P, TT, 4]), ALU.subtract))
            for t in range(TT):
                step(dve.tensor_tensor(prod[:, t], le[:, t], over(Gm[:, t, 0:4], 2, [P, 4, 8]), ALU.mult))
            step(dve.tensor_reduce(leg, prod.rearrange("p t g e -> p t e g"), AX, ALU.add))
            argmax_first(O1, leg, order8, 8, m1)
            step(dve.scalar_tensor_tensor(out=leg2, in0=O1, scalar=NEG, in1=leg, op0=ALU.mult, op1=ALU.add))
            argmax_first(O2, leg2, order8, 8, m2)
            dve.tensor_tensor(diff, m2, m1, ALU.subtract).then_inc(lexp_in, 1)
            dve.wait_ge(lexp_ready, 1)
            step(dve.tensor_reduce(pg, lexp, AX, ALU.add))
            step(dve.tensor_scalar(wa, diff, 1.0, None, ALU.add))
            step(dve.tensor_tensor(wa, wa, pg, ALU.mult))
            step(dve.reciprocal(wa, wa))
            step(dve.tensor_tensor(wb, wa, diff, ALU.mult))
            step(dve.tensor_tensor(cmb, O1, wa.to_broadcast([P, TT, 8]), ALU.mult))
            step(dve.tensor_tensor(tmp8, O2, wb.to_broadcast([P, TT, 8]), ALU.mult))
            step(dve.tensor_tensor(cmb, cmb, tmp8, ALU.add))
            dve.wait_ge(rank_done, 1)
            step(dve.tensor_copy(rank[:, :, 0:4], ps[:, 2:4, 0:4]))
            step(dve.tensor_scalar(cnt_over, ps[:, 2, 8:12], float(P), None, ALU.is_gt))
            step(dve.tensor_tensor(tmp4, Gm[:, :, 0:4], over(cnt_over, 1, [P, TT, 4]), ALU.mult))
            step(dve.tensor_reduce(Gm[:, :, 4:5], tmp4, AX, ALU.add))
            step(dve.tensor_tensor(tmp4, tmp4, rank[:, :, 0:4], ALU.mult))
            step(dve.tensor_reduce(rank[:, :, 4:5], tmp4, AX, ALU.add))
            step(dve.tensor_scalar(rank[:, :, 4:5], rank[:, :, 4:5], -float(P), None, ALU.add))
            step(dve.tensor_reduce(ov[:, 0:1], cnt_over, AX, ALU.add))
            step(dve.tensor_tensor(cnt_over, cnt_over, iota[:, 0:4], ALU.mult))
            step(dve.tensor_reduce(ov[:, 1:2], cnt_over, AX, ALU.add))
            step(dve.tensor_copy(flags[0:1, :], ov[0:1, :]))
            dve.sem_inc(routed, 1)

            def group_work(q):
                n0 = first_of(q)
                gcol, rcol = rt[:, 400:402], rt[:, 402:404]
                dve.tensor_copy(gcol.unsqueeze(2), Gm[:, :, bass.ds(q, 1)]).then_inc(grp_cols, 1)
                dve.tensor_copy(rcol.unsqueeze(2), rank[:, :, bass.ds(q, 1)]).then_inc(grp_cols, 1)
                dve.wait_ge(grp_cols, 2 * q + 2)
                for t in range(TT):
                    ins = dve.tensor_scalar(sel[:, t, :], iota[:, :], rcol[:, t:t + 1], gcol[:, t:t + 1],
                                            ALU.is_equal, ALU.mult)
                ins.then_inc(sel_ready, 1)
                dve.wait_ge(selT_done, q + 1)
                dve.tensor_copy(selT[:, :], ps[:, 7, 0:S]).then_inc(selT_ready, 1)
                wsel = rt[:, 408:416]
                dve.tensor_copy(wsel, ps[:, 7, S:S + EPG]).then_inc(selT_ready, 1)
                for r in range(4):
                    dve.wait_ge(xghi_ready, 4 * q + r + 1)
                    dve.tensor_tensor(xg_lo[:, 4 * r:4 * r + 4, :], ps[:, 5 + r % 2, :].rearrange("p (c t) -> p c t", c=4),
                                      xg_hi[:, 4 * r:4 * r + 4, :].bitcast(F32), ALU.subtract).then_inc(xglo_ready, 1)
                lo(n0 + 3, 0, 3)

                def h_mul(e):
                    dve.wait_ge(silu_ready, EPG * q + e + 1)
                    dve.scalar_tensor_tensor(out=hval[:, :], in0=ps[:, 4, F:2 * F], scalar=wsel[:, bass.ds(e, 1)],
                                             in1=hgate[:, :], op0=ALU.mult, op1=ALU.mult).then_inc(h_ready, 1)

                def hT_evac(e):
                    dve.wait_ge(hThi_ready, EPG * q + e + 1)
                    dve.tensor_tensor(hT_lo[:, :, :], ps[:, 7, 0:S].rearrange("p (f t) -> p f t", f=2),
                                      hT_hi[:, :, :].bitcast(F32), ALU.subtract).then_inc(hTlo_ready, 1)

                h_mul(0)
                with dve.Fori(1, EPG) as j:
                    base = n0 + 6 * j - 2
                    for c in range(4):
                        lo(base + c, (1 + c) % SPL, (4 + c) % RAW)
                        if c == 1:
                            hT_evac(j - 1)
                    for half in range(2):
                        lo(base + 4 + half, (2 + half) % SPL, 2 + half)
                    h_mul(j)
                for half in range(2):
                    lo(n0 + PER_GRP - 2 + half, (1 + half) % SPL, 4 + half)
                hT_evac(EPG - 1)
                dve.wait_ge(tile_used, n0 + PER_GRP)
                for nb in (1, 3):
                    dve.tensor_copy(yg[:, 512 * nb:512 * nb + 512], ps[:, nb, :]).then_inc(yg_ready, 1)
                for k in range(8):
                    t, nb = divmod(k, 4)
                    v = x1[:, t, 512 * nb:512 * nb + 512]
                    dve.wait_ge(scat_done, 8 * q + k + 1)
                    dve.tensor_tensor(v, v, ps[:, 5 + k % 2, :], ALU.add).then_inc(scat_added, 1)

            def group_lead(q):
                for i in range(LEAD):
                    lo(first_of(q) + i, i, i)

            group_work(0)
            with dve.Fori(1, NGRP) as q:
                group_lead(q)
                group_work(q)
            dve.wait_ge(scat_added, 8 * NGRP)
            overflow = dve.value_load(flags[0:1, 0:1], min_val=0, max_val=1)
            with dve.If(overflow > 0):
                group_lead(NGRP)
                group_work(NGRP)
                dve.wait_ge(scat_added, 8 * NGRP + 8)
            dve.sem_inc(all_added, 1)

        @block.tensor
        def _(pe):
            def used(ins):
                ins.then_inc(tile_used, 1)

            def split3(dst, l_hi, l_lo, r_hi, r_lo, start, stop):
                pe.matmul(dst, l_hi, r_hi, start=start, stop=False, skip_group_check=True)
                pe.matmul(dst, l_hi, r_lo, start=False, stop=False, skip_group_check=True)
                return pe.matmul(dst, l_lo, r_hi, start=False, stop=stop, skip_group_check=True)

            pe.wait_ge(masks_ready, 1)
            pe.wait_ge(small_in, 16 * N_SMALL)
            pe.transpose(ps[:, 0, 0:N_ROWS], rows[:, :], ident[0:N_ROWS, 0:N_ROWS]).then_inc(cols_done, 1)
            pe.wait_ge(xn_ready, 2)
            for i in range(8):
                if i >= 4:
                    pe.wait_ge(xlo_ready, i - 3)
                for k in range(2):
                    for t in range(TT):
                        ins = pe.transpose(ps[:, 4 + i % 4, k * S + t * P:k * S + t * P + P],
                                           xn[:, t, 2 * i + k::KC], ident[:, :])
                ins.then_inc(xpose_done, 1)
            pe.wait_ge(xlo_ready, 8)
            pe.wait_ge(wglo_ready, 1)
            pe.wait_ge(cols_ready, 1)

            def post(b):
                pe.wait_ge(znat_ready, 2 * b + 2)
                pe.wait_ge(zT_used, b + 1)
                for k in range(4):
                    for t in range(TT):
                        ins = pe.transpose(ps[:, 6 + k // 2, (k % 2) * S + t * P:(k % 2) * S + t * P + P],
                                           znat[:, t, P * k:P * k + P], ident[:, :])
                ins.then_inc(post_done, 1)

            with pe.Fori(0, 3) as i:
                for k in range(3):
                    b = 3 * i + k
                    for q in range(4):
                        place = 4 * k + q
                        pe.wait_ge(lo_ready, 12 * i + place + 1)
                        r_hi, r_lo = (tile_views(w[:, place % SPL, :], "rows") for w in (w_hi, w_lo))
                        for c in range(4):
                            for t in range(TT):
                                tk = slice(P * t, P * t + P)
                                ins = split3(ps[:, 2 * k + t, :], xT_hi[:, 4 * q + c, tk], xT_lo[:, 4 * q + c, tk],
                                             r_hi[:, c, :], r_lo[:, c, :], start=(q == 0 and c == 0),
                                             stop=(q == 3 and c == 3))
                                if q == 3 and c == 3:
                                    last = ins
                        used(ins)
                    if k:
                        post(b - 1)
                    if k == 2:
                        post(b)

            for t in range(TT):
                for c in range(KC):
                    tk = slice(P * t, P * t + P)
                    ins = split3(ps[:, 2 + t, 0:NGATE], xT_hi[:, c, tk], xT_lo[:, c, tk], wg_hi[:, c, :], wg_lo[:, c, :],
                                 start=(c == 0), stop=(c == KC - 1))
            ins.then_inc(gate_done, 1)
            pe.wait_ge(pooled_ready, 1)
            for g in range(4):
                ins = pe.matmul(ps[:, g // 2, (g % 2) * S:(g % 2) * S + S], poolw[:, g, :], pT[:, g, :],
                                start=True, stop=True)
            ins.then_inc(pooly_done, 1)
            pe.wait_ge(blklo_ready, 1)
            for kv in range(2):
                for q in range(4):
                    n = T_CMP + 4 * kv + q
                    pe.wait_ge(lo_ready, n + 1)
                    for l in range(8):
                        ins = split3(ps[0:2 * NC_, 4 + kv, 0:CH], blk_hi[:, kv, 8 * q + l, :], blk_lo[:, kv, 8 * q + l, :],
                                     w_hi[:, n % SPL, CH * l:CH * l + CH], w_lo[:, n % SPL, CH * l:CH * l + CH],
                                     start=(q == 0 and l == 0), stop=(q == 3 and l == 7))
                    used(ins)
            pe.wait_ge(hs_ready, 2)
            pe.wait_ge(zT_used, 10)
            for kv in range(2):
                for c in range(2):
                    ins = pe.transpose(ps[:, 6, 32 * (2 * kv + c):32 * (2 * kv + c) + 2 * NC_],
                                       hs[:, kv, P * c:P * c + P], ident[0:2 * NC_, 0:2 * NC_])
            ins.then_inc(hsT_done, 1)
            pe.wait_ge(hsT_ready, 1)
            for c in range(2):
                pe.matmul(ps[0:2 * NC_, 7, 0:HD], hsT[:, c, :], w2[:, 0, c, :], start=(c == 0), stop=(c == 1))
            for h in range(NKV):
                for c in range(2):
                    ins = pe.matmul(ps[0:NC_, 7, HD * (1 + h):HD * (2 + h)], hsT[:, 2 + c, NC_ * h:NC_ * h + NC_],
                                    w2[:, 1, c, :], start=(c == 0), stop=(c == 1))
            ins.then_inc(kcv_done, 1)
            pe.wait_ge(kcn_ready, 1)
            pe.transpose(ps[:, 6, 256:256 + 2 * NC_], kcn[:, :], ident[0:2 * NC_, 0:2 * NC_]).then_inc(kcT_done, 1)
            pe.wait_ge(kcT_ready, 1)
            pe.wait_ge(vc_ready, 1)
            pe.wait_ge(gexp_ready, 1)
            pe.wait_ge(convhi_ready, 1)

            def scores(j):
                u, kind = divmod(j, 3)
                kv, tt = divmod(u, 2)
                if j >= 3:
                    pe.wait_ge(prob_ready, j - 2)
                for h in range(G4):
                    q_ = qT[:, G4 * kv + h, P * tt:P * tt + P]
                    if kind == 2:
                        ins = pe.matmul(ps[:, 4, 16 * h:16 * h + NC_], q_, kcT[:, NC_ * kv:NC_ * kv + NC_],
                                        start=True, stop=True)
                    else:
                        n = P * (tt + 1)
                        ins = pe.matmul(ps[:, 2 * kind + h // 2, (h % 2) * S:(h % 2) * S + n], q_,
                                        kT[:, kind, kv, 0:n], start=True, stop=True)
                ins.then_inc(score_done, 1)

            def probs_T(j):
                tt, kind = (j // 3) % 2, j % 3
                pe.wait_ge(prob_ready, j + 1)
                if j:
                    pe.wait_ge(pt_ready, j)
                for h in range(G4):
                    if kind == 2:
                        ins = pe.transpose(ps[0:NC_, 5, P * h:P * h + P], prob[:, j % 2, h, 0:NC_], ident[:, :])
                    else:
                        for s in range(tt + 1):
                            ins = pe.transpose(ps[:, 5 + s, P * h:P * h + P], prob[:, j % 2, h, P * s:P * s + P],
                                               ident[:, :])
                ins.then_inc(pt_done, 1)

            def values(j):
                u, kind = divmod(j, 3)
                kv, tt = divmod(u, 2)
                pe.wait_ge(pt_ready, j + 1)
                if kind == 0 and u:
                    pe.wait_ge(olo_ready, u)
                if kind == 2:
                    ins = pe.matmul(ps[:, 7, :], vc[:, kv, :], pT_sb[0:NC_, j % 2, 0, :], start=False, stop=True)
                else:
                    for s in range(tt + 1):
                        ins = pe.matmul(ps[:, 7, :], vnat[:, s, kind, HD * kv:HD * kv + HD], pT_sb[:, j % 2, s, :],
                                        start=(kind == 0 and s == 0), stop=False)
                ins.then_inc(pv_done, 1)

            scores(0)
            scores(1)
            for j in range(12):
                probs_T(j)
                if j < 10:
                    scores(j + 2)
                values(j)

            pe.wait_ge(olo_ready, 4)
            for b in range(4):
                if b >= 2:
                    pe.wait_ge(x1_ready, b - 1)
                for q in range(4):
                    n = T_OUT + 4 * b + q
                    pe.wait_ge(lo_ready, n + 1)
                    r_hi, r_lo = (tile_views(w[:, n % SPL, :], "rows") for w in (w_hi, w_lo))
                    for c in range(4):
                        for t in range(TT):
                            tk = slice(P * t, P * t + P)
                            ins = split3(ps[:, 2 * (b % 2) + t, :], mix_hi[:, 4 * q + c, tk], mix_lo[:, 4 * q + c, tk],
                                         r_hi[:, c, :], r_lo[:, c, :], start=(q == 0 and c == 0), stop=(q == 3 and c == 3))
                    used(ins)

            pe.wait_ge(hn_ready, 2)
            pe.wait_ge(x1_ready, 4)
            for i in range(8):
                if i >= 4:
                    pe.wait_ge(hnTv_ready if i % 2 else hnTa_ready, (i - 4) // 2 + 1)
                for k in range(2):
                    for t in range(TT):
                        ins = pe.transpose(ps[:, 4 + i % 4, k * S + t * P:k * S + t * P + P],
                                           hn[:, t, 2 * i + k::KC], ident[:, :])
                ins.then_inc(hpose_done, 1)
            pe.wait_ge(hnTa_ready, 4)
            pe.wait_ge(hnTv_ready, 4)
            pe.wait_ge(rw36_ready, 2)
            for t in range(TT):
                for c in range(KC):
                    ins = pe.matmul(ps[:, t, 0:NGRP + NEXP], hnT[:, c, P * t:P * t + P], rw36[:, c, :],
                                    start=(c == 0), stop=(c == KC - 1))
            ins.then_inc(logit_done, 1)
            Gm = rt[:, 272:282].rearrange("p (t g) -> p t g", t=TT)
            cmb = rt[:, 256:272].rearrange("p (t e) -> p t e", t=TT)
            pe.wait_ge(onehot_ready, 1)
            pe.matmul(ps[:, 2, 0:4], upper[:, :], Gm[:, 0, 0:4], start=True, stop=True)
            pe.matmul(ps[:, 3, 0:4], ones[:, :], Gm[:, 0, 0:4], start=True, stop=False)
            pe.matmul(ps[:, 3, 0:4], upper[:, :], Gm[:, 1, 0:4], start=False, stop=True)
            pe.matmul(ps[:, 2, 8:12], ones[:, :], Gm[:, 0, 0:4], start=True, stop=False)
            pe.matmul(ps[:, 2, 8:12], ones[:, :], Gm[:, 1, 0:4], start=False, stop=True).then_inc(rank_done, 1)

            def group_work(q):
                n0 = first_of(q)
                pe.wait_ge(sel_ready, q + 1)
                for t in range(TT):
                    pe.transpose(ps[:, 7, P * t:P * t + P], sel[:, t, :], ident[:, :])
                for t in range(TT):
                    ins = pe.matmul(ps[:, 7, S:S + EPG], sel[:, t, :], cmb[:, t, :], start=(t == 0), stop=(t == 1))
                ins.then_inc(selT_done, 1)
                for r in range(4):
                    if r >= 2:
                        pe.wait_ge(xglo_ready, 4 * q + r - 1)
                    for c in range(4):
                        for t in range(TT):
                            ins = pe.matmul(ps[:, 5 + r % 2, P * c:P * c + P], hn[:, t, 4 * r + c::KC], sel[:, t, :],
                                            start=(t == 0), stop=(t == 1))
                    ins.then_inc(gather_done, 1)
                pe.wait_ge(xglo_ready, 4 * q + 4)
                pe.wait_ge(selT_ready, 2 * q + 2)
                for nb in range(4):
                    pe.matmul(ps[:, nb, :], zero_r[:, :], xg_hi[:, 0:4, :], start=True, stop=False, skip_group_check=True)

                def gate_up(n, place, c4):
                    pe.wait_ge(lo_ready, n + 1)
                    r_hi, r_lo = (tile_views(w[:, place % SPL, :], "gu") for w in (w_hi, w_lo))
                    for c in range(4):
                        ins = split3(ps[:, 4, :], xg_hi[:, 4 * c4 + c, :], xg_lo[:, 4 * c4 + c, :], r_hi[:, :, c, :],
                                     r_lo[:, :, c, :], start=(c4 == 0 and c == 0), stop=(c4 == 3 and c == 3))
                    used(ins)

                def hidden_T(e):
                    pe.wait_ge(h_ready, EPG * q + e + 1)
                    for f in range(2):
                        ins = pe.transpose(ps[:, 7, P * f:P * f + P], hval[:, f::2], ident[:, :])
                    ins.then_inc(hT_done, 1)

                def down(n, place, half):
                    pe.wait_ge(lo_ready, n + 1)
                    r_hi, r_lo = (tile_views(w[:, place % SPL, :], "down") for w in (w_hi, w_lo))
                    for k in range(2):
                        for f in range(2):
                            ins = split3(ps[:, 2 * half + k, :], hT_hi[:, f, :], hT_lo[:, f, :],
                                         r_hi[:, f, 512 * k:512 * k + 512], r_lo[:, f, 512 * k:512 * k + 512],
                                         start=False, stop=False)
                    used(ins)

                for c4 in range(4):
                    gate_up(n0 + c4, c4, c4)
                hidden_T(0)
                with pe.Fori(1, EPG) as j:
                    base = n0 + 6 * j - 2
                    for c4 in range(4):
                        gate_up(base + c4, 4 + c4, c4)
                        pe.wait_ge(hTlo_ready, EPG * q + j)
                    for half in range(2):
                        down(base + 4 + half, 2 + half, half)
                    hidden_T(j)
                pe.wait_ge(hTlo_ready, EPG * q + EPG)
                for half in range(2):
                    down(n0 + PER_GRP - 2 + half, 4 + half, half)
                pe.wait_ge(yg_ready, 4 * q + 4)
                for k in range(8):
                    t, nb = divmod(k, 4)
                    if k >= 2:
                        pe.wait_ge(scat_added, 8 * q + k - 1)
                    pe.matmul(ps[:, 5 + k % 2, :], selT[:, P * t:P * t + P], yg[:, 512 * nb:512 * nb + 512],
                              start=True, stop=True).then_inc(scat_done, 1)
                pe.wait_ge(scat_added, 8 * q + 8)

            pe.wait_ge(routed, 1)
            with pe.Fori(0, NGRP) as q:
                group_work(q)
            overflow = pe.value_load(flags[0:1, 0:1], min_val=0, max_val=1)
            with pe.If(overflow > 0):
                group_work(NGRP)


_PARAMS = ["norm1_w", "w_in", "pool_w", "pool_scale", "conv_w", "cmp_pe_k", "cmp_w1_k", "cmp_w2_k", "cmp_pe_v",
           "cmp_w1_v", "cmp_w2_v", "q_norm_w", "k_norm_w", "w_out", "norm2_w", "router_grp_w", "router_grp_b",
           "router_exp_w", "router_exp_b", "exp_w_gate", "exp_w_up", "exp_w_down"]


def build(nc, arrays):
    args = {n: nc.dram_tensor(f"in_{n}", a.shape, F32, kind="ExternalInput").ap() for n, a in arrays.items()}
    out = nc.dram_tensor("out_0", (S, D), F32, kind="ExternalOutput").ap()
    layer_kernel(nc, *args.values(), out)


def kernel(**inputs):
    import concourse.bacc as bacc
    from concourse.bass_utils import run_bass_kernel_spmd

    nc = bacc.Bacc("TRN2", target_bir_lowering=False, num_devices=1, dynamic_dma_scratch_size=1024)
    arrays = {"x": np.ascontiguousarray(inputs["x"])[0]}
    for name in _PARAMS:
        arrays[name] = np.ascontiguousarray(inputs[name])[0]
    arrays["pool_edge"] = np.array([[1.0 / min(t + 1, w) for t in range(16)] for w in WINDOWS], np.float32)
    build(nc, arrays)
    r = run_bass_kernel_spmd(nc, [{f"in_{n}": a for n, a in arrays.items()}], core_ids=[0])
    return r.results[0]["out_0"][None]
```

```python
from contextlib import ExitStack

import numpy as np

import concourse.bass as bass
from concourse import mybir

F32 = mybir.dt.float32
F32R = mybir.dt.float32r
I32 = mybir.dt.int32
ACT = mybir.ActivationFunctionType
ALU = mybir.AluOpType
AX = mybir.AxisListType.X

P = 128
S = 256
TT = S // P
D = 2048
KC = D // P
HD = 128
NH, NKV = 8, 2
G4 = NH // NKV
WINDOWS = (2, 4, 8, 16)
CMP_LEN, CMP_STRIDE = 32, 16
NC_ = (S - CMP_LEN) // CMP_STRIDE + 1
CH = 256
NGRP, EPG = 4, 8
NEXP = NGRP * EPG
F = 256
EPS = 1e-6
NEG = -1e30
SCALE = float(HD) ** -0.5

QA, QB, CC, KVS, KVW, CV, PU, KVC, CB = range(9)
BLOCK_COL = {QA: 2048, QB: 2560, CC: 1024, KVS: 3584, KVW: 4096, CV: 1536, PU: 0, KVC: 3072, CB: 512}
GATE_COL = 4608
NGATE = 3 * NH

TILE = 2048
RAW, SPL = 6, 3
N_IN, N_CMP, N_OUT = 36, 8, 16
T_CMP = N_IN
T_OUT = T_CMP + N_CMP
T_MOE = T_OUT + N_OUT
PER_GRP = 6 * EPG
LEAD = SPL

R_PE, R_CONV, R_PSC, R_QN, R_KN, N_ROWS = 0, 64, 76, 80, 81, 84
N_ROWLOADS = 6
N_SMALL = 10


def layer_kernel(nc, x, norm1_w, w_in, pool_w, pool_scale, conv_w, cmp_pe_k, cmp_w1_k, cmp_w2_k,
                 cmp_pe_v, cmp_w1_v, cmp_w2_v, q_norm_w, k_norm_w, w_out, norm2_w, router_grp_w,
                 router_grp_b, router_exp_w, router_exp_b, exp_w_gate, exp_w_up, exp_w_down, pool_edge, out):
    ctx = ExitStack()
    with ctx:
        def sem(name):
            return ctx.enter_context(nc.semaphore(name))

        def keep(name, shape, dt=F32):
            return ctx.enter_context(nc.sbuf_tensor(name, shape, dt))

        raw = keep("raw", [P, RAW, TILE])
        w_hi = keep("w_hi", [P, SPL, TILE], F32R)
        w_lo = keep("w_lo", [P, SPL, TILE], F32R)
        x1 = keep("x1", [P, TT, D])
        ident = keep("ident", [P, P])
        fold = keep("fold", [64, 32])
        causal = keep("causal", [P, P])
        cmask = keep("cmask", [P, 2, TT, NC_])
        upper = keep("upper", [P, P])
        ones = keep("ones", [P, P])
        iota = keep("iota", [P, P])
        edge = keep("edge", [P, 4, 16])
        rows = keep("rows", [N_ROWS, P])
        cols = keep("cols", [P, N_ROWS])
        w2 = keep("w2", [P, 2, 2, HD])
        gates = keep("gates", [P, TT, NGATE])
        rbias = keep("rbias", [P, NGRP + NEXP])
        st = keep("st", [P, 64])
        rgw = keep("rgw", [P, KC, NGRP])
        rew = keep("rew", [P, KC, NEXP])
        norm1c = keep("norm1c", [P, KC])
        norm2c = keep("norm2c", [P, KC])
        flags = keep("flags", [1, 2], I32)

        def phase(*tensors):
            with ExitStack() as es:
                return [es.enter_context(nc.sbuf_tensor(*t)) for t in tensors]

        def region(size, *phases):
            got = [phase(*p) for p in phases]
            ctx.enter_context(nc.sbuf_tensor(f"region{region.n}", [P, size // 4], F32))
            region.n += 1
            return got

        region.n = 0
        ((xT_hi, xT_lo), (blk_hi, blk_lo, prob, pT_sb), (_, x1T, junk), (hn, xg_hi, xg_lo)) = region(
            32768,
            [("xT_hi", [P, KC, S], F32R), ("xT_lo", [P, KC, S], F32R)],
            [("blk_hi", [P, 2, CMP_LEN, 2 * NC_], F32R), ("blk_lo", [P, 2, CMP_LEN, 2 * NC_], F32R),
             ("prob", [P, 2, G4, S], F32), ("pT_sb", [P, 2, TT, G4 * P], F32)],
            [("pad3", [P, TT * D], F32), ("x1T", [P, 2, 4, S], F32), ("junk", [P, 4, 512], F32)],
            [("hn", [P, TT, D], F32), ("xg_hi", [P, KC, P], F32R), ("xg_lo", [P, KC, P], F32R)],
        )
        ((xsq,), (kvcT, _, pA, pB, wg, etmp, _, work, wgt, gT), (_, blkf), (mix_hi, mix_lo),
         (yg_hi, yg_lo)) = region(
            32768,
            [("xsq", [P, TT, D], F32)],
            [("kvcT", [P, 4, S], F32), ("pad0", [P, 1024], F32), ("pA", [P, 4, S], F32), ("pB", [P, 4, S], F32),
             ("wg", [P, KC, 64], F32R), ("etmp", [P, 4, 16], F32), ("pad1", [P, 2048 - 1024 - 64], F32),
             ("work", [P, 4, S], F32), ("wgt", [P, KC, NGATE], F32), ("gT", [P, S], F32)],
            [("pad2", [P, 2048], F32), ("blkf", [P, 2, CMP_LEN, 2 * NC_], F32)],
            [("mix_hi", [P, KC, S], F32R), ("mix_lo", [P, KC, S], F32R)],
            [("yg_hi", [P, D], F32R), ("yg_lo", [P, D], F32R)],
        )
        ((qT,), (norm2b,), (sel, selT, hgate, hval, hT_hi, hT_lo)) = region(
            8192,
            [("qT", [P, NH, S], F32)],
            [("norm2b", [P, D], F32)],
            [("sel", [P, TT, P], F32), ("selT", [P, S], F32R), ("hgate", [P, F], F32), ("hval", [P, F], F32),
             ("hT_hi", [P, 2, P], F32R), ("hT_lo", [P, 2, P], F32R)],
        )
        ((kT, vnat, znat, cT, poolw, hs, hsT, vc, kcn, kcT, smx), (rt, rw36)) = region(
            23040,
            [("kT", [P, 2, NKV, S], F32), ("vnat", [P, TT, 2, NKV * HD], F32),
             ("znat", [P, TT, 512], F32), ("cT", [P, 4, S], F32),
             ("poolw", [P, 4, P], F32), ("hs", [2 * NC_, 2, CH], F32), ("hsT", [P, 4, 2 * NC_], F32),
             ("vc", [NC_, NKV, HD], F32), ("kcn", [2 * NC_, HD], F32), ("kcT", [P, 2 * NC_], F32),
             ("smx", [P, 3, 12, G4], F32)],
            [("rt", [P, 640], F32), ("rw36", [P, KC, NGRP + NEXP], F32)],
        )
        pT = cT
        ps = ctx.enter_context(nc.psum_tensor("ps", [P, 8, 512], F32))

        raw_in = [sem(f"raw_in{i}") for i in range(RAW)]
        half_hi_ready, half_lo_ready = sem("half_hi_ready"), sem("half_lo_ready")
        hi_ready, lo_ready, tile_used = sem("hi_ready"), sem("lo_ready"), sem("tile_used")
        x_in = [sem(f"x_in{t}") for t in range(TT)]
        norm1_in, rows_in, small_in, norm2_in = sem("norm1_in"), sem("rows_in"), sem("small_in"), sem("norm2_in")
        ident_ready, masks_ready = sem("ident_ready"), sem("masks_ready")
        pool_step, dve_step = sem("pool_step"), sem("dve_step")
        xsq_ready, xms_ready, xrt_ready, xrstd_ready = sem("xsq_ready"), sem("xms_ready"), sem("xrt_ready"), sem("xrstd_ready")
        xpose_done, xhi_ready, xlo_ready = sem("xpose_done"), sem("xhi_ready"), sem("xlo_ready")
        cols_done, cols_ready = sem("cols_done"), sem("cols_ready")
        znat_ready, post_done, zT_used = sem("znat_ready"), sem("post_done"), sem("zT_used")
        sq_ready, ms_ready, rt_ready = sem("sq_ready"), sem("ms_ready"), sem("rt_ready")
        v_kept = sem("v_kept")
        pooled_ready, pooly_done, poolhi_ready = sem("pooled_ready"), sem("pooly_done"), sem("poolhi_ready")
        convy_ready, convhi_ready = sem("convy_ready"), sem("convhi_ready")
        wghi_ready, wglo_ready, gate_done, gexp_ready = sem("wghi_ready"), sem("wglo_ready"), sem("gate_done"), sem("gexp_ready")
        gT_done, gT_ready, pool_kept, mixlo_ready = sem("gT_done"), sem("gT_ready"), sem("pool_kept"), sem("mixlo_ready")
        blkf_ready, blkhi_ready, blklo_ready = sem("blkf_ready"), sem("blkhi_ready"), sem("blklo_ready")
        hs_ready, hsT_done, hsT_ready = sem("hs_ready"), sem("hsT_done"), sem("hsT_ready")
        kcv_done, kcsq_ready, kcms_ready, kcrt_ready = sem("kcv_done"), sem("kcsq_ready"), sem("kcms_ready"), sem("kcrt_ready")
        kcn_ready, kcT_done, kcT_ready, vc_ready = sem("kcn_ready"), sem("kcT_done"), sem("kcT_ready"), sem("vc_ready")
        score_done, max_ready, exp_ready, prob_ready = sem("score_done"), sem("max_ready"), sem("exp_ready"), sem("prob_ready")
        pt_done, pt_ready, pv_done, ohi_ready, olo_ready = sem("pt_done"), sem("pt_ready"), sem("pv_done"), sem("ohi_ready"), sem("olo_ready")
        half_added, x1_ready = sem("half_added"), sem("x1_ready")
        ysq_ready, yms_ready, yrt_ready = sem("ysq_ready"), sem("yms_ready"), sem("yrt_ready")
        rstd_ready, x1w_ready, hn_ready = sem("rstd_ready"), sem("x1w_ready"), sem("hn_ready")
        x1pose_done, x1Ta_ready, x1Tv_ready, rw36_ready = sem("x1pose_done"), sem("x1Ta_ready"), sem("x1Tv_ready"), sem("rw36_ready")
        logit_done, lexp_in, lexp_ready = sem("logit_done"), sem("lexp_in"), sem("lexp_ready")
        onehot_ready, rank_done, rank_kept = sem("onehot_ready"), sem("rank_done"), sem("rank_kept")
        cmb_ready, routed = sem("cmb_ready"), sem("routed")
        grp_cols, sel_ready, selT_done, selT_ready = sem("grp_cols"), sem("sel_ready"), sem("selT_done"), sem("selT_ready")
        share_done, share_ready = sem("share_done"), sem("share_ready")
        gather_done, xghi_ready, xglo_ready = sem("gather_done"), sem("xghi_ready"), sem("xglo_ready")
        silu_ready, h_ready, hT_done = sem("silu_ready"), sem("h_ready"), sem("hT_done")
        hThi_ready, hTlo_ready, yghi_ready, yglo_ready = sem("hThi_ready"), sem("hTlo_ready"), sem("yghi_ready"), sem("yglo_ready")
        scat_done, scat_added, stored = sem("scat_done"), sem("scat_added"), sem("stored")

        xrstd = st[:, 6:8]

        col = lambda k: cols[:, k:k + 1]

        def over(ap, dim, shape):
            return ap.unsqueeze(dim).to_broadcast(shape)

        def tile_views(t, kind):
            if kind == "rows":
                return t.rearrange("p (c n) -> p c n", c=4)
            if kind == "gu":
                return t.rearrange("p (w c n) -> p w c n", w=2, c=4)
            return t.rearrange("p (f n) -> p f n", f=2)

        w_in_v = w_in.rearrange("(p c) n -> p c n", c=KC)
        w1_v = [w.rearrange("l d e -> d l e") for w in (cmp_w1_k, cmp_w1_v)]
        w_out_v = w_out.rearrange("(c p) n -> p c n", p=P)
        gate_v = exp_w_gate.rearrange("e (p c) n -> e p c n", c=KC)
        up_v = exp_w_up.rearrange("e (p c) n -> e p c n", c=KC)
        down_v = exp_w_down.rearrange("e (p f) n -> e p f n", f=2)
        out_v = out.rearrange("(t p) n -> p t n", p=P)

        def out_tile(i):
            return (i // 2, i % 2) if i < N_OUT // 2 else ((i - N_OUT // 2) // 2, 2 + i % 2)

        def first_of(q):
            return T_MOE + PER_GRP * q

        def gu_tiles(n0, e):
            return n0 + (4 if isinstance(e, int) and e == 0 else 6 * e + 2)

        block = ctx.enter_context(nc.Block())

        @block.sync
        def _(sp):
            def slot_free(n):
                sp.wait_ge(lo_ready, n - RAW + 1)

            sp.dma_start(norm1c[:, :], norm1_w.rearrange("(p c) -> p c", c=KC)).then_inc(norm1_in, 16)
            for t in range(TT):
                for half in range(2):
                    cs = slice(D // 2 * half, D // 2 * half + D // 2)
                    sp.dma_start(x1[:, t, cs], x[P * t:P * t + P, cs]).then_inc(x_in[t], 16)
            def load(dst, src):
                sp.dma_start(dst, src).then_inc(small_in, 16)

            for n in range(T_MOE):
                if n >= RAW:
                    slot_free(n)
                if n == 5:
                    load(edge[:, :, :], pool_edge.partition_broadcast(P))
                    load(w2[:, 0], cmp_w2_k.rearrange("(c p) d -> p c d", p=P))
                    load(w2[:, 1], cmp_w2_v.rearrange("(c p) d -> p c d", p=P))
                    load(wgt[:, :, :], w_in_v[:, :, GATE_COL:GATE_COL + NGATE])
                    load(rgw[:, :, :].rearrange("p (b c) g -> p b (c g)", b=4), router_grp_w.rearrange("(b p c) g -> p b (c g)", b=4, c=4))
                    load(rew[:, :, :].rearrange("p (b c) g -> p b (c g)", b=4), router_exp_w.rearrange("(b p c) g -> p b (c g)", b=4, c=4))
                    load(norm2c[:, :].rearrange("p (b c) -> p b c", b=4), norm2_w.rearrange("(b p c) -> p b c", b=4, c=4))
                    load(rbias[:, 0:NGRP], router_grp_b.partition_broadcast(P))
                    load(rbias[:, NGRP:], router_exp_b.partition_broadcast(P))
                    load(poolw[:, :, :], pool_w.rearrange("g c d -> c g d"))
                if n < T_CMP:
                    b, q = divmod(n, 4)
                    src = w_in_v[:, 4 * q:4 * q + 4, BLOCK_COL[b]:BLOCK_COL[b] + 512]
                elif n < T_OUT:
                    kv, q = divmod(n - T_CMP, 4)
                    src = w1_v[kv][:, 8 * q:8 * q + 8, :]
                else:
                    b, q = out_tile(n - T_OUT)
                    src = w_out_v[:, 4 * q:4 * q + 4, 512 * b:512 * b + 512]
                dst = raw[:, n % RAW, :]
                dst = dst.rearrange("p (l e) -> p l e", l=8) if T_CMP <= n < T_OUT else tile_views(dst, "rows")
                sp.dma_start(dst, src).then_inc(raw_in[n % RAW], 16)
            sp.wait_ge(olo_ready, 4)
            sp.dma_start(norm2b[:, :], norm2_w.partition_broadcast(P)).then_inc(norm2_in, 16)

            def load_gu(e, n, slot, c):
                slot_free(n)
                dst = tile_views(raw[:, slot, :], "gu")
                sp.dma_start(dst[:, 0], gate_v[e, :, 4 * c:4 * c + 4, :]).then_inc(raw_in[slot], 16)
                sp.dma_start(dst[:, 1], up_v[e, :, 4 * c:4 * c + 4, :]).then_inc(raw_in[slot], 16)

            def load_down(e, n, slot, half):
                slot_free(n)
                dst = tile_views(raw[:, slot, :], "down")
                for f in range(2):
                    sp.dma_start(dst[:, f, :], down_v[e, :, f, 1024 * half:1024 * half + 1024]).then_inc(raw_in[slot], 16)

            def group_loads(q, grp):
                n0 = first_of(q)
                for c in range(4):
                    load_gu(grp * EPG, n0 + c, c, c)
                with sp.Fori(1, EPG) as j:
                    for c in range(4):
                        load_gu(grp * EPG + j, n0 + 6 * j - 2 + c, (4 + c) % RAW, c)
                    for half in range(2):
                        load_down(grp * EPG + j - 1, n0 + 6 * j + 2 + half, 2 + half, half)
                for half in range(2):
                    load_down(grp * EPG + EPG - 1, n0 + PER_GRP - 2 + half, 4 + half, half)

            with sp.Fori(0, NGRP) as q:
                group_loads(q, q)
            sp.wait_ge(routed, 1)
            overflow = sp.value_load(flags[0:1, 0:1], min_val=0, max_val=1)
            full_group = sp.value_load(flags[0:1, 1:2], min_val=0, max_val=NGRP - 1)
            with sp.If(overflow > 0):
                group_loads(NGRP, full_group)
            for k, cs in ((4, slice(0, 1024)), (6, slice(1024, 1536)), (8, slice(1536, D))):
                sp.wait_ge(scat_added, 8 * NGRP - 8 + k + 8 * overflow)
                sp.dma_start(out_v[:, :, cs], x1[:, :, cs]).then_inc(stored, 16)
            sp.wait_ge(stored, 16 * 3)

        @block.gpsimd
        def _(pool):
            steps = [0]

            def step(ins):
                steps[0] += 1
                ins.then_inc(pool_step, 1)
                pool.wait_ge(pool_step, steps[0])

            step(pool.memset(ident[:, :], 0.0))
            step(pool.affine_select(out=ident[:, :], in_=ident[:, :], compare_op=ALU.not_equal, fill=1.0,
                                    base=0, pattern=[[-1, P]], channel_multiplier=1))
            pool.sem_inc(ident_ready, 1)
            step(pool.memset(fold[:, :], 0.0))
            for k in range(2):
                step(pool.affine_select(out=fold[:, :], in_=fold[:, :], compare_op=ALU.not_equal, fill=1.0,
                                        base=-32 * k, pattern=[[-1, 32]], channel_multiplier=1))
            step(pool.memset(ones[:, :], 1.0))
            step(pool.memset(wg[:, :, :].bitcast(F32), 0.0))
            step(pool.memset(causal[:, :], 0.0))
            step(pool.affine_select(out=causal[:, :], in_=causal[:, :], compare_op=ALU.is_ge, fill=NEG,
                                    base=0, pattern=[[-1, P]], channel_multiplier=1))
            step(pool.affine_select(out=upper[:, :], in_=ones[:, :], compare_op=ALU.is_ge, fill=0.0,
                                    base=-1, pattern=[[1, P]], channel_multiplier=-1))
            for k, fill in ((0, NEG), (1, 0.0)):
                step(pool.memset(cmask[:, k, :, :], float(k)))
                step(pool.affine_select(out=cmask[:, k, :, :], in_=cmask[:, k, :, :], compare_op=ALU.is_ge,
                                        fill=fill, base=1 - CMP_LEN, pattern=[[P, TT], [-CMP_STRIDE, NC_]],
                                        channel_multiplier=1))
            pool.iota(iota[:, :], pattern=[[1, P]], base=0, channel_multiplier=0,
                      allow_small_or_imprecise_dtypes=True).then_inc(masks_ready, 1)
            for i, b in enumerate((KVS, KVW)):
                pool.wait_ge(znat_ready, 2 * (b + 1))
                pool.tensor_copy(vnat[:, :, i, :], znat[:, :, 256:512]).then_inc(v_kept, 1)

        @block.scalar
        def _(act):
            def load(dst, src, signal):
                act.dma_start(dst, src).then_inc(signal, 16)

            load(rows[R_QN:R_KN, :], q_norm_w.unsqueeze(0), rows_in)
            load(rows[R_KN:N_ROWS, :], k_norm_w, rows_in)
            load(rows[R_PE:R_PE + 32, :], cmp_pe_k, rows_in)
            load(rows[R_PE + 32:R_PE + 64, :], cmp_pe_v, rows_in)
            load(rows[R_CONV:R_PSC, :], conv_w.rearrange("k (j p) -> (k j) p", p=P), rows_in)
            load(rows[R_PSC:R_QN, :], pool_scale.rearrange("(g p) -> g p", p=P), rows_in)

            def hi(n, slot=None, rslot=None, count=None):
                slot = n % SPL if slot is None else slot
                rslot = n % RAW if rslot is None else rslot
                act.wait_ge(raw_in[rslot], 16 * (n // RAW + 1) if count is None else count)
                if count is not None or n >= SPL:
                    act.wait_ge(tile_used, n - SPL + 1)
                act.activation(w_hi[:, slot, :], raw[:, rslot, :], ACT.Copy).then_inc(hi_ready, 1)

            act.wait_ge(norm1_in, 16)
            act.activation(st[:, 60:61], norm1c[:, 0:1], ACT.Copy)
            for c in range(KC):
                if c % 2 == 0:
                    act.wait_ge(xpose_done, c // 2 + 1)
                ins = act.activation(xT_hi[:, c, :], ps[:, c // 2, (c % 2) * S:(c % 2) * S + S], ACT.Copy,
                                     scale=norm1c[:, c:c + 1])
                if c % 2:
                    ins.then_inc(xhi_ready, 1)
                if c == 11:
                    hi(1)
                if c == 5:
                    act.wait_ge(raw_in[0], 16)
                    act.activation(w_hi[:, 0, 0:TILE // 2], raw[:, 0, 0:TILE // 2], ACT.Copy).then_inc(half_hi_ready, 1)
                    act.activation(w_hi[:, 0, TILE // 2:], raw[:, 0, TILE // 2:], ACT.Copy).then_inc(hi_ready, 1)
                    act.wait_ge(cols_done, 1)
                    act.activation(cols[:, :], ps[:, 0, 0:N_ROWS], ACT.Copy).then_inc(cols_ready, 1)
            for t in range(TT):
                ins = act.activation(xsq[:, t, :], x1[:, t, :], ACT.Square, accum_out=st[:, t:t + 1])
            ins.then_inc(xsq_ready, 1)
            hi(2)
            act.wait_ge(xms_ready, 1)
            act.activation(st[:, 4:6], st[:, 2:4], ACT.Sqrt).then_inc(xrt_ready, 1)
            act.wait_ge(xrstd_ready, 1)

            n_norm = [0]

            def z_evac(b):
                z = ps[:, 2 * (b % 3):2 * (b % 3) + 2, :]
                act.wait_ge(tile_used, 4 * b + 4)
                if b in (QA, QB, KVS, KVW):
                    w = 512 if b in (QA, QB) else 256
                    if n_norm[0]:
                        act.wait_ge(ms_ready, n_norm[0])
                    sq = work[:, :, :].rearrange("p a b -> p (a b)")
                    for t in range(TT):
                        ins = act.activation(sq[:, w * t:w * t + w], z[:, t, 0:w], ACT.Square, scale=xrstd[:, t:t + 1])
                    ins.then_inc(sq_ready, 1)
                    n_norm[0] += 1
                    if w == 256:
                        act.wait_ge(post_done, b)
                        if b == KVW:
                            act.wait_ge(v_kept, 1)
                        for t in range(TT):
                            ins = act.activation(znat[:, t, 256:512], z[:, t, 256:512], ACT.Copy, scale=xrstd[:, t:t + 1])
                        ins.then_inc(znat_ready, 1)
                    act.wait_ge(ms_ready, n_norm[0])
                    act.activation(st[:, 16:16 + w // 64], st[:, 8:8 + w // 64], ACT.Sqrt).then_inc(rt_ready, 1)
                    return
                act.wait_ge(post_done, b)
                if b == CV:
                    act.wait_ge(v_kept, 2)
                act.activation(znat[:, 0, :], z[:, 0, :], ACT.Copy, scale=xrstd[:, 0:1]).then_inc(znat_ready, 1)

            def zT_evac(b):
                zT = ps[:, 6:8, :].rearrange("p b (h t) -> p (b h) t", h=2)
                if b in (CV, CB):
                    return
                act.wait_ge(post_done, b + 1)
                if b in (QA, QB):
                    act.activation(qT[:, 4 * b:4 * b + 4, :], zT, ACT.Copy, scale=col(R_QN)).then_inc(zT_used, 1)
                elif b == CC:
                    act.activation(cT[:, :, :], zT, ACT.Copy).then_inc(zT_used, 1)
                elif b in (KVS, KVW):
                    k = b - KVS
                    act.activation(kT[:, k, :, :], zT[:, 0:2, :], ACT.Copy, scale=col(R_KN + 1 + k)).then_inc(zT_used, 1)
                elif b == PU:
                    act.activation(pT[:, :, :], zT, ACT.Copy).then_inc(zT_used, 1)
                elif b == KVC:
                    act.activation(kvcT[:, :, :], zT, ACT.Copy).then_inc(zT_used, 1)

            for n in range(3, T_CMP + 2):
                hi(n)
                if n == 9:
                    act.wait_ge(small_in, 16 * N_SMALL)
                    act.wait_ge(masks_ready, 1)
                    act.activation(wg[:, :, 0:NGATE], wgt[:, :, :], ACT.Copy).then_inc(wghi_ready, 1)
                if n >= 5 and n % 4 == 1:
                    b = (n - 5) // 4
                    z_evac(b)
                    if b:
                        zT_evac(b - 1)

            def exps(j):
                tt, kind = (j // 3) % 2, j % 3
                n = NC_ if kind == 2 else P * (tt + 1)
                act.wait_ge(max_ready, j + 1)
                if j >= 2:
                    act.wait_ge(pt_done, j - 1)
                for h in range(G4):
                    s = ps[:, 4, 16 * h:16 * h + n] if kind == 2 else \
                        ps[:, h // 2, (h % 2) * S:(h % 2) * S + n]
                    act.activation(prob[:, j % 2, h, 0:n], s, ACT.Exp, bias=smx[:, 0, j, h:h + 1],
                                   accum_out=smx[:, 1, j, h:h + 1]).then_inc(exp_ready, 1)

            def pt_evac(j):
                tt, kind = (j // 3) % 2, j % 3
                act.wait_ge(pt_done, j + 1)
                if j >= 2:
                    act.wait_ge(pv_done, j - 1)
                if kind == 2:
                    act.activation(pT_sb[0:NC_, j % 2, 0, :], ps[0:NC_, 4, :], ACT.Copy).then_inc(pt_ready, 1)
                else:
                    act.activation(pT_sb[:, j % 2, 0:tt + 1, :], ps[:, 5:6 + tt, :], ACT.Copy).then_inc(pt_ready, 1)

            def o_hi(u):
                kv, tt = divmod(u, 2)
                act.wait_ge(pv_done, 3 * (u + 1))
                act.activation(mix_hi[:, 8 + G4 * kv:8 + G4 * kv + G4, P * tt:P * tt + P],
                               ps[:, 7, :].rearrange("p (h t) -> p h t", h=G4), ACT.Copy).then_inc(ohi_ready, 1)

            act.wait_ge(gT_done, 1)
            act.activation(gT[0:64, :], ps[0:64, 2, 0:S], ACT.Copy).then_inc(gT_ready, 1)
            act.wait_ge(blkf_ready, 1)
            for kv in range(2):
                act.activation(blk_hi[:, kv], blkf[:, kv], ACT.Copy).then_inc(blkhi_ready, 1)
            act.wait_ge(pooly_done, 1)
            for g in range(4):
                act.activation(mix_hi[:, g, :], ps[:, g // 2, (g % 2) * S:(g % 2) * S + S], ACT.Copy,
                               scale=col(R_PSC + g)).then_inc(poolhi_ready, 1)
            act.wait_ge(gate_done, 1)
            for t in range(TT):
                ins = act.activation(gates[:, t, :], ps[:, 3, 32 * t:32 * t + NGATE], ACT.Exp, scale=st[:, 2 + t:3 + t])
            ins.then_inc(gexp_ready, 1)
            act.wait_ge(convy_ready, 1)
            act.activation(mix_hi[:, 4:8, :], work[:, :, :], ACT.Copy).then_inc(convhi_ready, 1)
            hi(T_CMP + 2)

            exps(0)
            for n in range(T_CMP + 3, T_CMP + 7):
                hi(n)
            pt_evac(0)
            exps(1)
            for n in range(T_CMP + 7, T_OUT + 2):
                hi(n)
            act.wait_ge(tile_used, T_OUT)
            act.activation(hs[:, :, :].rearrange("p k e -> p (k e)"), ps[0:2 * NC_, 4, :], ACT.Silu).then_inc(hs_ready, 1)
            act.wait_ge(hsT_done, 1)
            act.activation(hsT[:, :, :], ps[:, 6, 0:128].rearrange("p (k n) -> p k n", k=4)[:, :, 0:2 * NC_],
                           ACT.Copy).then_inc(hsT_ready, 1)
            pt_evac(1)
            act.wait_ge(kcv_done, 1)
            act.activation(kcn[:, :], ps[0:2 * NC_, 6, HD:2 * HD], ACT.Square, accum_out=st[0:2 * NC_, 24:25]).then_inc(kcsq_ready, 1)
            act.wait_ge(kcms_ready, 1)
            act.activation(st[0:2 * NC_, 26:27], st[0:2 * NC_, 25:26], ACT.Sqrt).then_inc(kcrt_ready, 1)
            hi(T_OUT + 2)
            act.wait_ge(kcT_done, 1)
            act.activation(kcT[:, :], ps[:, 4, 0:2 * NC_], ACT.Copy, scale=col(R_KN)).then_inc(kcT_ready, 1)
            exps(2)
            exps(3)
            hi(T_OUT + 3)
            pt_evac(2)
            o_hi(0)

            for u in range(1, 4):
                j = 3 * u
                pt_evac(j)
                exps(j + 1)
                exps(j + 2)
                hi(T_OUT + 2 * u + 2)
                pt_evac(j + 1)
                pt_evac(j + 2)
                if u < 3:
                    exps(j + 3)
                hi(T_OUT + 2 * u + 3)
                o_hi(u)
            hi(T_OUT + N_OUT // 2 + 2)

            def squares(b):
                act.wait_ge(x1_ready, b + 1)
                if b >= 2:
                    act.wait_ge(x1Ta_ready, b - 1)
                for t in range(TT):
                    ins = act.activation(junk[:, 2 * (b % 2) + t, :], x1[:, t, 512 * b:512 * b + 512], ACT.Square,
                                         accum_out=st[:, 32 + 4 * t + b:33 + 4 * t + b])
                return ins

            def x1T_evac(b):
                act.wait_ge(x1pose_done, b + 1)
                act.activation(x1T[:, b % 2, 0:2, :], ps[:, 4, :].rearrange("p (c t) -> p c t", c=2),
                               ACT.Copy).then_inc(x1Ta_ready, 1)

            for b in range(4):
                m = T_OUT + 8 + 2 * b
                hi(m + 3, count=None if m + 3 < T_MOE else 160 + 32)
                if b:
                    x1T_evac(b - 1)
                if b < 3:
                    hi(m + 4, count=None if m + 4 < T_MOE else 160 + 32)
                    squares(b)

            squares(3).then_inc(ysq_ready, 1)
            x1T_evac(3)
            act.wait_ge(yms_ready, 1)
            act.activation(st[:, 46:48], st[:, 44:46], ACT.Sqrt).then_inc(yrt_ready, 1)
            act.wait_ge(rstd_ready, 1)
            act.wait_ge(x1w_ready, 4)
            for t in range(TT):
                act.activation(hn[:, t, :], hn[:, t, :], ACT.Copy, scale=st[:, 58 + t:59 + t]).then_inc(hn_ready, 1)
            hi(T_MOE + LEAD - 1, count=160 + 32)

            def router_exps():
                act.wait_ge(lexp_in, 1)
                act.activation(rt[:, 80:90], rt[:, 80:90], ACT.Exp).then_inc(lexp_ready, 1)

            def ring_hi(q):
                def at(p):
                    hi(first_of(q) + p, slot=p % SPL, rslot=p % RAW, count=160 + 32 * EPG * q + 32 * (p // RAW + 1))
                return at

            def gathered(q, r):
                act.wait_ge(gather_done, 4 * q + r + 1)
                act.activation(xg_hi[:, 4 * r:4 * r + 4, :],
                               ps[:, 5 + r % 2, :].rearrange("p (c t) -> p c t", c=4), ACT.Copy).then_inc(xghi_ready, 1)

            def silu(q, e, last_tile):
                act.wait_ge(tile_used, first_of(q) + last_tile + 1)
                act.activation(hgate[:, :], ps[:, 4, 0:F], ACT.Silu).then_inc(silu_ready, 1)

            def hT_evac(q, e):
                act.wait_ge(hT_done, EPG * q + e + 1)
                act.activation(hT_hi[:, :, :], ps[:, 7, 0:S].rearrange("p (f t) -> p f t", f=2),
                               ACT.Copy).then_inc(hThi_ready, 1)

            def first_expert(q, router=False):
                at = ring_hi(q)
                gathered(q, 0)
                gathered(q, 1)
                if router:
                    router_exps()
                at(3)
                gathered(q, 2)
                at(4)
                gathered(q, 3)
                at(5)
                silu(q, 0, 3)
                hT_evac(q, 0)
                at(6)

            def other_experts(q, into_next):
                n0, at = first_of(q), ring_hi(q)
                for p in range(7, 10):
                    at(p)
                silu(q, 1, 7)
                with act.Fori(2, EPG - 1) as j:
                    for c in range(6):
                        hi(n0 + 6 * j - 2 + c, slot=(1 + c) % SPL, rslot=(4 + c) % RAW,
                           count=160 + 32 * EPG * q + 32 * (j if c < 2 else j + 1))
                        if c == 1:
                            hT_evac(q, j - 1)
                    silu(q, j, 6 * j + 1)
                for p in range(40, 46):
                    at(p)
                    if p == 41:
                        hT_evac(q, EPG - 2)
                silu(q, EPG - 1, 43)
                if into_next:
                    gathered(q + 1, 0)
                    gathered(q + 1, 1)
                    at(46)
                    gathered(q + 1, 2)
                    at(47)
                    hT_evac(q, EPG - 1)
                    gathered(q + 1, 3)
                    for p in range(48, 51):
                        at(p)
                else:
                    at(46)
                    hT_evac(q, EPG - 1)
                    at(47)
                for nb in range(4):
                    if nb % 2 == 0:
                        act.wait_ge(tile_used, n0 + PER_GRP - 1 + nb // 2)
                    act.activation(yg_hi[:, 512 * nb:512 * nb + 512], ps[:, nb, :], ACT.Copy).then_inc(yghi_ready, 1)
                if into_next:
                    for p in range(51, 54):
                        at(p)
                    silu(q + 1, 0, 3)
                    hT_evac(q + 1, 0)
                    at(54)

            first_expert(0, router=True)
            with act.Fori(0, NGRP - 1) as q:
                other_experts(q, True)
            other_experts(NGRP - 1, False)
            act.wait_ge(routed, 1)
            overflow = act.value_load(flags[0:1, 0:1], min_val=0, max_val=1)
            with act.If(overflow > 0):
                for p in range(LEAD):
                    ring_hi(NGRP)(p)
                first_expert(NGRP)
                other_experts(NGRP, False)

        @block.vector
        def _(dve):
            steps = [0]

            def step(ins):
                steps[0] += 1
                ins.then_inc(dve_step, 1)
                dve.wait_ge(dve_step, steps[0])

            def lo(n, slot=None, rslot=None):
                slot = n % SPL if slot is None else slot
                rslot = n % RAW if rslot is None else rslot
                dve.wait_ge(hi_ready, n + 1)
                dve.tensor_tensor(w_lo[:, slot, :], raw[:, rslot, :], w_hi[:, slot, :].bitcast(F32),
                                  ALU.subtract).then_inc(lo_ready, 1)

            for c in range(KC):
                if c % 2 == 0:
                    dve.wait_ge(xhi_ready, c // 2 + 1)
                ins = dve.scalar_tensor_tensor(out=xT_lo[:, c, :], in0=ps[:, c // 2, (c % 2) * S:(c % 2) * S + S],
                                               scalar=norm1c[:, c:c + 1], in1=xT_hi[:, c, :].bitcast(F32),
                                               op0=ALU.mult, op1=ALU.subtract)
                if c % 2:
                    ins.then_inc(xlo_ready, 1)
                if c == 11:
                    lo(1)
                if c == 5:
                    for half, (got, done) in enumerate(((half_hi_ready, half_lo_ready), (hi_ready, lo_ready))):
                        hs_ = slice(TILE // 2 * half, TILE // 2 * half + TILE // 2)
                        dve.wait_ge(got, 1)
                        dve.tensor_tensor(w_lo[:, 0, hs_], raw[:, 0, hs_], w_hi[:, 0, hs_].bitcast(F32),
                                          ALU.subtract).then_inc(done, 1)
            dve.wait_ge(cols_ready, 1)
            dve.tensor_scalar(col(R_QN), col(R_QN), SCALE, None, ALU.mult).then_inc(zT_used, 1)
            dve.wait_ge(xsq_ready, 1)
            dve.tensor_scalar(st[:, 2:4], st[:, 0:2], 1.0 / D, EPS, ALU.mult, ALU.add).then_inc(xms_ready, 1)
            lo(2)
            dve.wait_ge(xrt_ready, 1)
            step(dve.reciprocal(xrstd, st[:, 4:6]))
            step(dve.tensor_scalar(st[:, 2:4], xrstd, -1.0, None, ALU.mult))
            dve.sem_inc(xrstd_ready, 1)

            n_norm = [0]

            def z_evac(b):
                z = ps[:, 2 * (b % 3):2 * (b % 3) + 2, :]
                if b in (QA, QB, KVS, KVW):
                    w = 512 if b in (QA, QB) else 256
                    nh = w // HD
                    n_norm[0] += 1
                    dve.wait_ge(sq_ready, n_norm[0])
                    sq = work[:, :, :].rearrange("p a b -> p (a b)")[:, 0:2 * w]
                    step(dve.tensor_reduce(st[:, 48:48 + 2 * nh], sq.rearrange("p (h d) -> p h d", d=HD), AX, ALU.add))
                    dve.tensor_scalar(st[:, 8:8 + 2 * nh], st[:, 48:48 + 2 * nh], 1.0 / HD, EPS, ALU.mult,
                                      ALU.add).then_inc(ms_ready, 1)
                    dve.wait_ge(rt_ready, n_norm[0])
                    step(dve.reciprocal(st[:, 24:24 + 2 * nh], st[:, 16:16 + 2 * nh]))
                    rr = st[:, 24:24 + 2 * nh].rearrange("p (t h) -> p t h", t=TT)
                    step(dve.tensor_tensor(rr, rr, over(xrstd, 2, [P, TT, nh]), ALU.mult))
                    if b:
                        dve.wait_ge(post_done, b)
                    if b == KVW:
                        dve.wait_ge(v_kept, 1)
                    for t in range(TT):
                        r = st[:, 24 + nh * t:24 + nh * t + nh]
                        ins = dve.tensor_tensor(znat[:, t, 0:w].rearrange("p (h d) -> p h d", d=HD),
                                                z[:, t, 0:w].rearrange("p (h d) -> p h d", d=HD),
                                                over(r, 2, [P, nh, HD]), ALU.mult)
                        if w == 512 or t:
                            ins.then_inc(znat_ready, 1)
                    return
                dve.wait_ge(tile_used, 4 * b + 4)
                dve.wait_ge(post_done, b)
                if b == CV:
                    dve.wait_ge(v_kept, 2)
                dve.tensor_scalar(znat[:, 1, :], z[:, 1, :], xrstd[:, 1:2], None, ALU.mult).then_inc(znat_ready, 1)

            zT = ps[:, 6:8, :].rearrange("p b (h t) -> p (b h) t", h=2)

            def after_v():
                dve.wait_ge(post_done, CV + 1)
                dve.wait_ge(zT_used, CC + 2)
                step(dve.tensor_tensor(cT[:, :, :], zT, cT[:, :, :], ALU.mult))
                dve.sem_inc(zT_used, 1)
                for j in range(4):
                    step(dve.tensor_scalar(work[:, j, :], cT[:, j, :], col(R_CONV + 8 + j), None, ALU.mult))
                    for shift, k in ((1, 1), (2, 0)):
                        step(dve.scalar_tensor_tensor(out=work[:, j, shift:], in0=cT[:, j, 0:S - shift],
                                                      scalar=col(R_CONV + 4 * k + j), in1=work[:, j, shift:],
                                                      op0=ALU.mult, op1=ALU.add))

            def pool_sums():
                dve.wait_ge(zT_used, PU + 2)
                src, dst = pT, pA
                for level, shift in enumerate((1, 2, 4, 8)):
                    g = slice(level, 4)
                    dve.tensor_copy(dst[:, g, 0:shift], src[:, g, 0:shift])
                    step(dve.tensor_tensor(dst[:, g, shift:], src[:, g, shift:], src[:, g, 0:S - shift], ALU.add))
                    src, dst = dst, (pB if dst is pA else pA)

            def pool_means():
                for g, w in enumerate(WINDOWS):
                    s = pA if g % 2 == 0 else pB
                    step(dve.tensor_tensor(etmp[:, g, :], s[:, g, 0:16], edge[:, g, :], ALU.mult))
                    step(dve.tensor_tensor(etmp[:, g, :], etmp[:, g, :], pT[:, g, 0:16], ALU.subtract))
                    step(dve.scalar_tensor_tensor(out=pT[:, g, :], in0=s[:, g, :], scalar=1.0 / w, in1=pT[:, g, :],
                                                  op0=ALU.mult, op1=ALU.subtract))
                dve.tensor_copy(pT[:, :, 0:16], etmp[:, :, :]).then_inc(pooled_ready, 1)

            def after_kvc():
                dve.wait_ge(zT_used, KVC + 2)
                for kv in range(2):
                    for lh in range(2):
                        for h in range(NKV):
                            src = kvcT[:, 2 * kv + h, :].rearrange("p (n l) -> p n l", l=CMP_STRIDE)[:, lh:lh + NC_, :]
                            pe = cols[:, R_PE + 32 * kv + 16 * lh:R_PE + 32 * kv + 16 * lh + 16]
                            dst = blkf[:, kv, 16 * lh:16 * lh + 16, NC_ * h:NC_ * h + NC_].rearrange("p l n -> p n l")
                            ins = dve.tensor_tensor(dst, src, over(pe, 1, [P, NC_, CMP_STRIDE]), ALU.add)
                ins.then_inc(blkf_ready, 1)

            for n in range(3, T_CMP + 2):
                lo(n)
                if n == 9:
                    dve.wait_ge(wghi_ready, 1)
                    dve.tensor_tensor(wg[:, :, 32:32 + NGATE], wgt[:, :, :], wg[:, :, 0:NGATE].bitcast(F32),
                                      ALU.subtract).then_inc(wglo_ready, 1)
                if n >= 5 and n % 4 == 1:
                    b = (n - 5) // 4
                    z_evac(b)
                    if b == CV + 1:
                        after_v()
                    if b == PU + 1:
                        pool_sums()
                if n == T_CMP - 1:
                    pool_means()
            after_kvc()
            dve.wait_ge(post_done, CB + 1)
            step(dve.tensor_tensor(work[:, :, :], zT, work[:, :, :], ALU.mult))
            dve.sem_inc(zT_used, 1)
            dve.sem_inc(convy_ready, 1)
            for kv in range(2):
                dve.wait_ge(blkhi_ready, kv + 1)
                dve.tensor_tensor(blk_lo[:, kv], blkf[:, kv], blk_hi[:, kv].bitcast(F32), ALU.subtract).then_inc(blklo_ready, 1)
            for g in range(4):
                dve.wait_ge(poolhi_ready, 2 * (g // 2) + 2)
                ins = dve.scalar_tensor_tensor(out=mix_lo[:, g, :], in0=ps[:, g // 2, (g % 2) * S:(g % 2) * S + S],
                                               scalar=col(R_PSC + g), in1=mix_hi[:, g, :].bitcast(F32),
                                               op0=ALU.mult, op1=ALU.subtract)
            ins.then_inc(pool_kept, 1)
            dve.wait_ge(gexp_ready, 1)
            step(dve.tensor_scalar(gates[:, :, :], gates[:, :, :], 1.0, None, ALU.add))
            step(dve.reciprocal(gates[:, :, :], gates[:, :, :]))

            dve.wait_ge(masks_ready, 1)

            def score_view(j, n):
                if j % 3 == 2:
                    return ps[:, 4, 0:64].rearrange("p (h n) -> p h n", h=G4)[:, :, 0:n]
                return ps[:, 0:2, :].rearrange("p b (h s) -> p (b h) s", h=2)[:, :, 0:n]

            def mask_max(j):
                tt, kind = (j // 3) % 2, j % 3
                dve.wait_ge(score_done, j + 1)
                if kind == 2:
                    s = score_view(j, NC_)
                    step(dve.tensor_tensor(s, s, over(cmask[:, 0, tt, :], 1, [P, G4, NC_]), ALU.add))
                else:
                    s = score_view(j, P * (tt + 1))
                    d = s[:, :, P * tt:P * tt + P]
                    step(dve.tensor_tensor(d, d, over(causal[:, :], 1, [P, G4, P]), ALU.add))
                dve.tensor_reduce(smx[:, 0, j, :], s, AX, ALU.max, negate=True).then_inc(max_ready, 1)

            def scale_probs(j):
                u, kind = divmod(j, 3)
                kv, tt = divmod(u, 2)
                n = NC_ if kind == 2 else P * (tt + 1)
                dve.wait_ge(exp_ready, 4 * (j + 1))
                step(dve.reciprocal(smx[:, 2, j, :], smx[:, 1, j, :]))
                g0 = NH * (0 if kind == 2 else kind + 1) + G4 * kv
                step(dve.tensor_tensor(smx[:, 2, j, :], smx[:, 2, j, :], gates[:, tt, g0:g0 + G4], ALU.mult))
                p = prob[:, j % 2, :, 0:n]
                ins = dve.tensor_tensor(p, p, over(smx[:, 2, j, :], 2, [P, G4, n]), ALU.mult)
                if kind == 2:
                    step(ins)
                    ins = dve.tensor_tensor(p, p, over(cmask[:, 1, tt, :], 1, [P, G4, NC_]), ALU.mult)
                ins.then_inc(prob_ready, 1)

            def o_lo(u):
                kv, tt = divmod(u, 2)
                dve.wait_ge(ohi_ready, u + 1)
                hs_ = slice(8 + G4 * kv, 8 + G4 * kv + G4)
                dve.tensor_tensor(mix_lo[:, hs_, P * tt:P * tt + P], ps[:, 7, :].rearrange("p (h t) -> p h t", h=G4),
                                  mix_hi[:, hs_, P * tt:P * tt + P].bitcast(F32), ALU.subtract).then_inc(olo_ready, 1)

            def half_add(b):
                dve.wait_ge(tile_used, T_OUT + 2 * b + 2)
                v = x1[:, :, 512 * b:512 * b + 512]
                dve.tensor_tensor(v, v, ps[:, 2:4, :], ALU.add).then_inc(half_added, 1)

            mask_max(0)
            lo(T_CMP + 2)
            scale_probs(0)
            for n in range(T_CMP + 3, T_CMP + 7):
                lo(n)
            mask_max(1)
            dve.wait_ge(convhi_ready, 1)
            dve.tensor_tensor(mix_lo[:, 4:8, :], work[:, :, :], mix_hi[:, 4:8, :].bitcast(F32), ALU.subtract).then_inc(mixlo_ready, 1)
            scale_probs(1)
            for n in range(T_CMP + 7, T_OUT + 2):
                lo(n)
            dve.wait_ge(kcsq_ready, 1)
            dve.tensor_scalar(st[0:2 * NC_, 25:26], st[0:2 * NC_, 24:25], 1.0 / HD, EPS, ALU.mult, ALU.add).then_inc(kcms_ready, 1)
            dve.tensor_copy(vc[:, :, :], ps[0:NC_, 6, 2 * HD:4 * HD].rearrange("p (h d) -> p h d", h=2)).then_inc(vc_ready, 1)
            dve.wait_ge(kcrt_ready, 1)
            step(dve.reciprocal(st[0:2 * NC_, 27:28], st[0:2 * NC_, 26:27]))
            dve.tensor_scalar(kcn[:, :], ps[0:2 * NC_, 6, HD:2 * HD], st[0:2 * NC_, 27:28], None, ALU.mult).then_inc(kcn_ready, 1)
            lo(T_OUT + 2)
            mask_max(2)
            mask_max(3)
            scale_probs(2)
            scale_probs(3)
            lo(T_OUT + 3)
            half_add(0)

            for u in range(1, 4):
                j = 3 * u
                mask_max(j + 1)
                mask_max(j + 2)
                if u == 1:
                    o_lo(0)
                scale_probs(j + 1)
                scale_probs(j + 2)
                lo(T_OUT + 2 * u + 2)
                if u < 3:
                    mask_max(j + 3)
                    scale_probs(j + 3)
                half_add(u)
                lo(T_OUT + 2 * u + 3)
                o_lo(u)
            lo(T_OUT + N_OUT // 2 + 2)

            dve.wait_ge(small_in, 16 * N_SMALL)
            for w, cs in ((rgw, slice(0, NGRP)), (rew, slice(NGRP, NGRP + NEXP))):
                ins = dve.tensor_tensor(rw36[:, :, cs], w[:, :, :], over(norm2c[:, :], 2, list(w.shape)), ALU.mult)
            ins.then_inc(rw36_ready, 1)

            def x1_add(b):
                dve.wait_ge(tile_used, T_OUT + 8 + 2 * b + 2)
                dve.wait_ge(half_added, 4)
                v = x1[:, :, 512 * b:512 * b + 512]
                dve.tensor_tensor(v, v, ps[:, 2 * (b % 2):2 * (b % 2) + 2, :], ALU.add).then_inc(x1_ready, 1)

            def x1_weighted(b):
                cs = slice(512 * b, 512 * b + 512)
                dve.wait_ge(x1_ready, b + 1)
                dve.wait_ge(norm2_in, 16)
                dve.tensor_tensor(hn[:, :, cs], x1[:, :, cs], over(norm2b[:, cs], 1, [P, TT, 512]), ALU.mult).then_inc(x1w_ready, 1)

            def x1T_evac(b):
                dve.wait_ge(x1pose_done, b + 1)
                dve.tensor_copy(x1T[:, b % 2, 2:4, :], ps[:, 5, :].rearrange("p (c t) -> p c t", c=2)).then_inc(x1Tv_ready, 1)

            for b in range(4):
                m = T_OUT + 8 + 2 * b
                lo(m + 3)
                if b:
                    x1T_evac(b - 1)
                x1_add(b)
                if b < 3:
                    lo(m + 4)
                    x1_weighted(b)

            x1_weighted(3)
            dve.wait_ge(ysq_ready, 1)
            step(dve.tensor_reduce(st[:, 40:42], st[:, 32:40].rearrange("p (t b) -> p t b", t=TT), AX, ALU.add))
            dve.tensor_scalar(st[:, 44:46], st[:, 40:42], 1.0 / D, EPS, ALU.mult, ALU.add).then_inc(yms_ready, 1)
            x1T_evac(3)
            dve.wait_ge(yrt_ready, 1)
            rstd = st[:, 58:60]
            step(dve.reciprocal(rstd, st[:, 46:48]))
            dve.sem_inc(rstd_ready, 1)

            def rv(a, *dims):
                n = TT * int(np.prod(dims))
                v = rt[:, a:a + n]
                if len(dims) == 2:
                    return v.rearrange("p (t a b) -> p t a b", t=TT, a=dims[0])
                return v.rearrange("p (t a) -> p t a", t=TT)

            L = rv(0, 36)
            gmax, lexp = rv(72, 1), rv(80, 4)
            diff = rv(88, 1)
            tie, pg = rv(92, 4), rv(100, 1)
            prod, leg, leg2 = rv(104, 4, 8), rv(168, 8), rv(184, 8)
            m1, m2, E, O1, O2 = rv(200, 1), rv(202, 1), rv(204, 8), rv(220, 8), rv(236, 8)
            wa, wb = rv(252, 1), rv(254, 1)
            cmb = rv(256, 8)
            Gm, rank = rv(272, 5), rv(282, 5)
            cnt_over, tmp4, ov = rt[:, 292:296], rv(296, 4), rt[:, 304:306]
            tied, order8, order4 = rv(306, 1), rt[:, 320:328], rt[:, 328:332]
            tmp8 = rv(332, 8)

            step(dve.tensor_scalar(order8, iota[:, 0:8], -1.0, 8.0, ALU.mult, ALU.add))
            step(dve.tensor_scalar(order4, iota[:, 0:4], -1.0, 4.0, ALU.mult, ALU.add))
            dve.wait_ge(logit_done, 1)
            for t in range(TT):
                step(dve.scalar_tensor_tensor(out=L[:, t], in0=ps[:, 6 + t, 0:36], scalar=rstd[:, t:t + 1], in1=rbias[:, :],
                                              op0=ALU.mult, op1=ALU.add))
            lg = L[:, :, 0:4]
            le = L[:, :, 4:36].rearrange("p t (g e) -> p t g e", g=NGRP)

            def argmax_first(one_hot, values, order, n, top):
                step(dve.tensor_reduce(top, values, AX, ALU.max))
                step(dve.tensor_tensor(E[:, :, 0:n], values, top.to_broadcast([P, TT, n]), ALU.is_equal))
                step(dve.tensor_tensor(E[:, :, 0:n], E[:, :, 0:n], over(order, 1, [P, TT, n]), ALU.mult))
                step(dve.tensor_reduce(tied, E[:, :, 0:n], AX, ALU.max))
                step(dve.tensor_tensor(one_hot, E[:, :, 0:n], tied.to_broadcast([P, TT, n]), ALU.is_equal))

            argmax_first(Gm[:, :, 0:4], lg, order4, 4, gmax)
            dve.sem_inc(onehot_ready, 1)
            for t in range(TT):
                step(dve.tensor_tensor(prod[:, t], le[:, t], over(Gm[:, t, 0:4], 2, [P, 4, 8]), ALU.mult))
            step(dve.tensor_reduce(leg, prod.rearrange("p t g e -> p t e g"), AX, ALU.add))
            dve.wait_ge(rank_done, 1)
            before = rt[:, 344:360]
            step(dve.tensor_copy(before, ps[:, 2, 0:16]))
            dve.sem_inc(rank_kept, 1)
            dve.tensor_copy(rank[:, 0, 0:4], before[:, 0:4])
            step(dve.tensor_tensor(rank[:, 1, 0:4], before[:, 4:8], before[:, 8:12], ALU.add))

            def count_tokens():
                step(dve.tensor_tensor(cnt_over, before[:, 8:12], before[:, 12:16], ALU.add))
                step(dve.tensor_scalar(cnt_over, cnt_over, float(P), None, ALU.is_gt))
                step(dve.tensor_tensor(tmp4, Gm[:, :, 0:4], over(cnt_over, 1, [P, TT, 4]), ALU.mult))
                step(dve.tensor_reduce(Gm[:, :, 4:5], tmp4, AX, ALU.add))
                step(dve.tensor_tensor(tmp4, tmp4, rank[:, :, 0:4], ALU.mult))
                step(dve.tensor_reduce(rank[:, :, 4:5], tmp4, AX, ALU.add))
                step(dve.tensor_scalar(rank[:, :, 4:5], rank[:, :, 4:5], -float(P), None, ALU.add))
                step(dve.tensor_reduce(ov[:, 0:1], cnt_over, AX, ALU.add))
                step(dve.tensor_tensor(cnt_over, cnt_over, iota[:, 0:4], ALU.mult))
                step(dve.tensor_reduce(ov[:, 1:2], cnt_over, AX, ALU.add))
                step(dve.tensor_copy(flags[0:1, :], ov[0:1, :]))
                dve.sem_inc(routed, 1)

            def top_two():
                argmax_first(O1, leg, order8, 8, m1)
                step(dve.scalar_tensor_tensor(out=leg2, in0=O1, scalar=NEG, in1=leg, op0=ALU.mult, op1=ALU.add))
                argmax_first(O2, leg2, order8, 8, m2)
                step(dve.tensor_tensor(lexp, lg, gmax.to_broadcast([P, TT, 4]), ALU.subtract))
                dve.tensor_tensor(diff, m2, m1, ALU.subtract).then_inc(lexp_in, 1)

            def expert_weights():
                dve.wait_ge(lexp_ready, 1)
                step(dve.tensor_reduce(pg, lexp, AX, ALU.add))
                step(dve.tensor_scalar(wa, diff, 1.0, None, ALU.add))
                step(dve.tensor_tensor(wa, wa, pg, ALU.mult))
                step(dve.reciprocal(wa, wa))
                step(dve.tensor_tensor(wb, wa, diff, ALU.mult))
                step(dve.tensor_tensor(cmb, O1, wa.to_broadcast([P, TT, 8]), ALU.mult))
                step(dve.tensor_tensor(tmp8, O2, wb.to_broadcast([P, TT, 8]), ALU.mult))
                step(dve.tensor_tensor(cmb, cmb, tmp8, ALU.add))
                dve.sem_inc(cmb_ready, 1)

            shares = rt[:, 408:416]

            def make_sel(q):
                if isinstance(q, int):
                    gcol, rcol = Gm[:, :, q], rank[:, :, q]
                else:
                    gcol, rcol = rt[:, 400:402], rt[:, 402:404]
                    dve.tensor_copy(gcol.unsqueeze(2), Gm[:, :, bass.ds(q, 1)]).then_inc(grp_cols, 1)
                    dve.tensor_copy(rcol.unsqueeze(2), rank[:, :, bass.ds(q, 1)]).then_inc(grp_cols, 1)
                    dve.wait_ge(grp_cols, 2 * q - 2)
                for t in range(TT):
                    ins = dve.tensor_scalar(sel[:, t, :], iota[:, :], rcol[:, t:t + 1], gcol[:, t:t + 1],
                                            ALU.is_equal, ALU.mult)
                ins.then_inc(sel_ready, 1)

            def take_shares(q):
                if not (isinstance(q, int) and q == 0):
                    dve.wait_ge(h_ready, EPG * q)
                dve.wait_ge(share_done, q + 1)
                dve.tensor_copy(shares, ps[:, 7, S:S + EPG]).then_inc(share_ready, 1)

            def take_selT(q):
                dve.wait_ge(selT_done, q + 1)
                dve.tensor_copy(selT[:, :], ps[:, 5, 0:S]).then_inc(selT_ready, 1)

            def gathered(q, r):
                dve.wait_ge(xghi_ready, 4 * q + r + 1)
                dve.tensor_tensor(xg_lo[:, 4 * r:4 * r + 4, :], ps[:, 5 + r % 2, :].rearrange("p (c t) -> p c t", c=4),
                                  xg_hi[:, 4 * r:4 * r + 4, :].bitcast(F32), ALU.subtract).then_inc(xglo_ready, 1)

            def h_mul(q, e):
                dve.wait_ge(silu_ready, EPG * q + e + 1)
                dve.scalar_tensor_tensor(out=hval[:, :], in0=ps[:, 4, F:2 * F], scalar=shares[:, bass.ds(e, 1)],
                                         in1=hgate[:, :], op0=ALU.mult, op1=ALU.mult).then_inc(h_ready, 1)

            def hT_evac(q, e):
                dve.wait_ge(hThi_ready, EPG * q + e + 1)
                dve.tensor_tensor(hT_lo[:, :, :], ps[:, 7, 0:S].rearrange("p (f t) -> p f t", f=2),
                                  hT_hi[:, :, :].bitcast(F32), ALU.subtract).then_inc(hTlo_ready, 1)

            def add_back(q, k):
                nb, t = divmod(k, 2)
                v = x1[:, t, 512 * nb:512 * nb + 512]
                dve.wait_ge(scat_done, 8 * q + k + 1)
                dve.tensor_tensor(v, v, ps[:, 5 + k % 2, :], ALU.add).then_inc(scat_added, 1)

            def ring_lo(q):
                return lambda p: lo(first_of(q) + p, p % SPL, p % RAW)

            def first_expert(q, between=((),) * 4):
                at = ring_lo(q)

                def router_work(k):
                    for work_ in between[k]:
                        work_()

                gathered(q, 0)
                router_work(0)
                gathered(q, 1)
                router_work(1)
                at(3)
                gathered(q, 2)
                router_work(2)
                at(4)
                gathered(q, 3)
                router_work(3)
                at(5)
                take_shares(q)
                dve.wait_ge(share_ready, q + 1)
                h_mul(q, 0)
                hT_evac(q, 0)
                at(6)
                at(7)
                take_selT(q)

            def other_experts(q, into_next):
                n0, at = first_of(q), ring_lo(q)
                for p in range(8, 10):
                    at(p)
                h_mul(q, 1)
                with dve.Fori(2, EPG - 1) as j:
                    for c in range(6):
                        lo(n0 + 6 * j - 2 + c, (1 + c) % SPL, (4 + c) % RAW)
                        if c == 1:
                            hT_evac(q, j - 1)
                    h_mul(q, j)
                for p in range(40, 46):
                    at(p)
                    if p == 41:
                        hT_evac(q, EPG - 2)
                h_mul(q, EPG - 1)
                if into_next:
                    take_shares(q + 1)
                    gathered(q + 1, 0)
                    gathered(q + 1, 1)
                    at(46)
                    gathered(q + 1, 2)
                    at(47)
                    hT_evac(q, EPG - 1)
                    gathered(q + 1, 3)
                    for p in range(48, 51):
                        at(p)
                else:
                    at(46)
                    hT_evac(q, EPG - 1)
                    at(47)

                def yg_evac(nb):
                    dve.wait_ge(yghi_ready, 4 * q + nb + 1)
                    dve.tensor_tensor(yg_lo[:, 512 * nb:512 * nb + 512], ps[:, nb, :],
                                      yg_hi[:, 512 * nb:512 * nb + 512].bitcast(F32), ALU.subtract).then_inc(yglo_ready, 1)

                yg_evac(0)
                yg_evac(1)
                if into_next:
                    yg_evac(2)
                    yg_evac(3)
                    at(51)
                    add_back(q, 0)
                    add_back(q, 1)
                    at(52)
                    add_back(q, 2)
                    add_back(q, 3)
                    h_mul(q + 1, 0)
                    at(53)
                    add_back(q, 4)
                    add_back(q, 5)
                    hT_evac(q + 1, 0)
                    at(54)
                    add_back(q, 6)
                    add_back(q, 7)
                    at(55)
                    take_selT(q + 1)
                    make_sel(q + 2)
                else:
                    for k in range(4):
                        add_back(q, k)
                    yg_evac(2)
                    yg_evac(3)
                    for k in range(4, 8):
                        add_back(q, k)

            make_sel(0)
            first_expert(0, between=((top_two,), (lambda: lo(T_MOE + LEAD - 1),), (count_tokens,), (expert_weights,)))
            make_sel(1)
            with dve.Fori(0, NGRP - 1) as q:
                other_experts(q, True)
            other_experts(NGRP - 1, False)
            overflow = dve.value_load(flags[0:1, 0:1], min_val=0, max_val=1)
            with dve.If(overflow > 0):
                for p in range(LEAD):
                    ring_lo(NGRP)(p)
                first_expert(NGRP)
                other_experts(NGRP, False)

        @block.tensor
        def _(pe):
            def used(ins):
                ins.then_inc(tile_used, 1)

            def split3(dst, l_hi, l_lo, r_hi, r_lo, start, stop):
                pe.matmul(dst, l_hi, r_hi, start=start, stop=False, skip_group_check=True)
                pe.matmul(dst, l_hi, r_lo, start=False, stop=False, skip_group_check=True)
                return pe.matmul(dst, l_lo, r_hi, start=False, stop=stop, skip_group_check=True)

            pe.wait_ge(ident_ready, 1)
            for t in range(TT):
                pe.wait_ge(x_in[t], 32)
                for i in range(8):
                    for k in range(2):
                        ins = pe.transpose(ps[:, i, k * S + t * P:k * S + t * P + P], x1[:, t, 2 * i + k::KC], ident[:, :])
                    if t == TT - 1:
                        ins.then_inc(xpose_done, 1)
            pe.wait_ge(xlo_ready, 1)
            pe.wait_ge(rows_in, 16 * N_ROWLOADS)
            pe.transpose(ps[:, 0, 0:N_ROWS], rows[:, :], ident[0:N_ROWS, 0:N_ROWS]).then_inc(cols_done, 1)

            def post(b):
                pe.wait_ge(znat_ready, 2 * b + 2)
                pe.wait_ge(zT_used, b + 1)
                for k in range(4):
                    for t in range(TT):
                        ins = pe.transpose(ps[:, 6 + k // 2, (k % 2) * S + t * P:(k % 2) * S + t * P + P],
                                           znat[:, t, P * k:P * k + P], ident[:, :])
                ins.then_inc(post_done, 1)

            def project(b, k):
                for q in range(4):
                    if isinstance(b, int) and b == 0:
                        pe.wait_ge(xlo_ready, 2 * q + 2)
                    place = 4 * k + q
                    first_tile = isinstance(b, int) and b == 0 and q == 0
                    if first_tile:
                        pe.wait_ge(half_lo_ready, 1)
                    else:
                        pe.wait_ge(lo_ready, 4 * b + q + 1)
                    r_hi, r_lo = (tile_views(w[:, place % SPL, :], "rows") for w in (w_hi, w_lo))
                    for c in range(4):
                        if first_tile and c == 2:
                            pe.wait_ge(lo_ready, 1)
                        for t in range(TT):
                            tk = slice(P * t, P * t + P)
                            ins = split3(ps[:, 2 * k + t, :], xT_hi[:, 4 * q + c, tk], xT_lo[:, 4 * q + c, tk],
                                         r_hi[:, c, :], r_lo[:, c, :], start=(q == 0 and c == 0),
                                         stop=(q == 3 and c == 3))
                    used(ins)

            pe.wait_ge(cols_ready, 1)
            project(0, 0)
            with pe.Fori(0, 2) as i:
                for k in range(1, 4):
                    project(3 * i + k, k % 3)
                    post(3 * i + k - 1)
            project(7, 1)
            post(6)
            project(8, 2)
            post(7)
            pe.wait_ge(wglo_ready, 1)
            for c in range(KC):
                pe.matmul(ps[0:64, 2, 0:S], wg[:, c, :], xT_hi[:, c, :], start=(c == 0), stop=False, skip_group_check=True)
                ins = pe.matmul(ps[0:32, 2, 0:S], wg[:, c, 0:32], xT_lo[:, c, :], start=False, stop=(c == KC - 1),
                                skip_group_check=True)
            ins.then_inc(gT_done, 1)
            post(8)

            pe.wait_ge(pooled_ready, 1)
            for g in range(4):
                ins = pe.matmul(ps[:, g // 2, (g % 2) * S:(g % 2) * S + S], poolw[:, g, :], pT[:, g, :],
                                start=True, stop=True)
            ins.then_inc(pooly_done, 1)
            pe.wait_ge(gT_ready, 1)
            for t in range(TT):
                ins = pe.matmul(ps[:, 3, 32 * t:32 * t + NGATE], gT[0:64, P * t:P * t + P], fold[:, 0:NGATE],
                                start=True, stop=True)
            ins.then_inc(gate_done, 1)

            def scores(j):
                u, kind = divmod(j, 3)
                kv, tt = divmod(u, 2)
                last = {0: j - 2, 1: j - 1, 2: j - 3}[kind]
                if last >= 0:
                    pe.wait_ge(exp_ready, 4 * (last + 1))
                if kind == 2 and last >= 0:
                    pe.wait_ge(pt_ready, last + 1)
                for h in range(G4):
                    q_ = qT[:, G4 * kv + h, P * tt:P * tt + P]
                    if kind == 2:
                        ins = pe.matmul(ps[:, 4, 16 * h:16 * h + NC_], q_, kcT[:, NC_ * kv:NC_ * kv + NC_],
                                        start=True, stop=True)
                    else:
                        n = P * (tt + 1)
                        ins = pe.matmul(ps[:, h // 2, (h % 2) * S:(h % 2) * S + n], q_,
                                        kT[:, kind, kv, 0:n], start=True, stop=True)
                ins.then_inc(score_done, 1)

            def probs_T(j):
                tt, kind = (j // 3) % 2, j % 3
                pe.wait_ge(prob_ready, j + 1)
                last = {0: j - 2, 1: j - 1, 2: j - 3}[kind]
                if last >= 0:
                    pe.wait_ge(pt_ready, last + 1)
                for h in range(G4):
                    if kind == 2:
                        ins = pe.transpose(ps[0:NC_, 4, P * h:P * h + P], prob[:, j % 2, h, 0:NC_], ident[:, :])
                    else:
                        for s in range(tt + 1):
                            ins = pe.transpose(ps[:, 5 + s, P * h:P * h + P], prob[:, j % 2, h, P * s:P * s + P],
                                               ident[:, :])
                ins.then_inc(pt_done, 1)

            def values(j):
                u, kind = divmod(j, 3)
                kv, tt = divmod(u, 2)
                pe.wait_ge(pt_ready, j + 1)
                if kind == 0 and u:
                    pe.wait_ge(olo_ready, u)
                if kind == 2:
                    ins = pe.matmul(ps[:, 7, :], vc[:, kv, :], pT_sb[0:NC_, j % 2, 0, :], start=False, stop=True)
                else:
                    for s in range(tt + 1):
                        ins = pe.matmul(ps[:, 7, :], vnat[:, s, kind, HD * kv:HD * kv + HD], pT_sb[:, j % 2, s, :],
                                        start=(kind == 0 and s == 0), stop=False)
                ins.then_inc(pv_done, 1)

            def out_sums(i):
                n = T_OUT + i
                b, q = out_tile(i)
                pe.wait_ge(lo_ready, n + 1)
                r_hi, r_lo = (tile_views(w[:, n % SPL, :], "rows") for w in (w_hi, w_lo))
                bank = 2 if q < 2 else 2 * (b % 2)
                for c in range(4):
                    for t in range(TT):
                        tk = slice(P * t, P * t + P)
                        ins = split3(ps[:, bank + t, :], mix_hi[:, 4 * q + c, tk], mix_lo[:, 4 * q + c, tk],
                                     r_hi[:, c, :], r_lo[:, c, :], start=(q % 2 == 0 and c == 0), stop=(q % 2 == 1 and c == 3))
                used(ins)

            def compress(kv, tiles=range(4)):
                for q in tiles:
                    n = T_CMP + 4 * kv + q
                    pe.wait_ge(lo_ready, n + 1)
                    for l in range(8):
                        ins = split3(ps[0:2 * NC_, 4, CH * kv:CH * kv + CH], blk_hi[:, kv, 8 * q + l, :], blk_lo[:, kv, 8 * q + l, :],
                                     w_hi[:, n % SPL, CH * l:CH * l + CH], w_lo[:, n % SPL, CH * l:CH * l + CH],
                                     start=(q == 0 and l == 0), stop=(q == 3 and l == 7))
                    used(ins)

            pe.wait_ge(blklo_ready, 1)
            compress(0, range(1))
            pe.wait_ge(pool_kept, 1)
            scores(0)
            compress(0, range(1, 4))
            scores(1)
            probs_T(0)
            pe.wait_ge(blklo_ready, 2)
            compress(1, range(1))
            values(0)
            compress(1, range(1, 4))
            pe.wait_ge(hs_ready, 1)
            pe.wait_ge(zT_used, 10)
            for kv in range(2):
                for c in range(2):
                    ins = pe.transpose(ps[:, 6, 32 * (2 * kv + c):32 * (2 * kv + c) + 2 * NC_],
                                       hs[:, kv, P * c:P * c + P], ident[0:2 * NC_, 0:2 * NC_])
            ins.then_inc(hsT_done, 1)
            probs_T(1)
            pe.wait_ge(hsT_ready, 1)
            for c in range(2):
                pe.matmul(ps[0:2 * NC_, 6, HD:2 * HD], hsT[:, c, :], w2[:, 0, c, :], start=(c == 0), stop=(c == 1))
            for h in range(NKV):
                for c in range(2):
                    ins = pe.matmul(ps[0:NC_, 6, HD * (2 + h):HD * (3 + h)], hsT[:, 2 + c, NC_ * h:NC_ * h + NC_],
                                    w2[:, 1, c, :], start=(c == 0), stop=(c == 1))
            ins.then_inc(kcv_done, 1)
            pe.wait_ge(mixlo_ready, 1)
            pe.wait_ge(gexp_ready, 1)
            out_sums(0)
            pe.wait_ge(kcn_ready, 1)
            pe.transpose(ps[:, 4, 0:2 * NC_], kcn[:, :], ident[0:2 * NC_, 0:2 * NC_]).then_inc(kcT_done, 1)
            values(1)
            pe.wait_ge(kcT_ready, 1)
            pe.wait_ge(vc_ready, 1)
            scores(2)
            scores(3)
            out_sums(1)
            probs_T(2)

            for u in range(1, 4):
                j = 3 * u
                scores(j + 1)
                scores(j + 2)
                if u == 1:
                    values(2)
                probs_T(j)
                pe.wait_ge(half_added, u)
                out_sums(2 * u)
                values(j)
                probs_T(j + 1)
                probs_T(j + 2)
                if u < 3:
                    scores(j + 3)
                out_sums(2 * u + 1)
                values(j + 1)
                values(j + 2)

            def x1_transposed(b):
                pe.wait_ge(x1_ready, b + 1)
                if b:
                    pe.wait_ge(x1Ta_ready, b)
                    pe.wait_ge(x1Tv_ready, b)
                for c in range(4):
                    for t in range(TT):
                        ins = pe.transpose(ps[:, 4 + c // 2, (c % 2) * S + t * P:(c % 2) * S + t * P + P],
                                           x1[:, t, 512 * b + c:512 * b + 512:4], ident[:, :])
                ins.then_inc(x1pose_done, 1)

            def logits(b):
                pe.wait_ge(x1Ta_ready, b + 1)
                pe.wait_ge(x1Tv_ready, b + 1)
                pe.wait_ge(rw36_ready, 1)
                for t in range(TT):
                    for c in range(4):
                        ins = pe.matmul(ps[:, 6 + t, 0:NGRP + NEXP], x1T[:, b % 2, c, P * t:P * t + P], rw36[:, 4 * b + c, :],
                                        start=(b == 0 and c == 0), stop=(b == 3 and c == 3))
                return ins

            pe.wait_ge(olo_ready, 4)
            pe.wait_ge(half_added, 4)
            for b in range(4):
                if b >= 2:
                    pe.wait_ge(x1_ready, b - 1)
                out_sums(8 + 2 * b)
                if b:
                    x1_transposed(b - 1)
                out_sums(9 + 2 * b)
                if b:
                    logits(b - 1)

            x1_transposed(3)
            logits(3).then_inc(logit_done, 1)
            Gm = rt[:, 272:282].rearrange("p (t g) -> p t g", t=TT)
            cmb = rt[:, 256:272].rearrange("p (t e) -> p t e", t=TT)
            pe.wait_ge(onehot_ready, 1)
            both = Gm[:, :, 0:4]
            pe.matmul(ps[:, 2, 0:8], upper[:, :], both, start=True, stop=True)
            pe.matmul(ps[:, 2, 8:16], ones[:, :], both, start=True, stop=True).then_inc(rank_done, 1)

            def take_shares(q):
                pe.wait_ge(sel_ready, q + 1)
                for t in range(TT):
                    ins = pe.matmul(ps[:, 7, S:S + EPG], sel[:, t, :], cmb[:, t, :], start=(t == 0), stop=(t == 1))
                ins.then_inc(share_done, 1)

            def gather(q, r):
                if r >= 2:
                    pe.wait_ge(xglo_ready, 4 * q + r - 1)
                for c in range(4):
                    for t in range(TT):
                        ins = pe.matmul(ps[:, 5 + r % 2, P * c:P * c + P], hn[:, t, 4 * r + c::KC], sel[:, t, :],
                                        start=(t == 0), stop=(t == 1))
                ins.then_inc(gather_done, 1)

            def transpose_sel():
                for t in range(TT):
                    ins = pe.transpose(ps[:, 5, P * t:P * t + P], sel[:, t, :], ident[:, :])
                ins.then_inc(selT_done, 1)

            def scatter(q, k):
                nb, t = divmod(k, 2)
                if t == 0:
                    pe.wait_ge(yglo_ready, 4 * q + nb + 1)
                if k >= 2:
                    pe.wait_ge(scat_added, 8 * q + k - 1)
                row, cs = selT[:, P * t:P * t + P], slice(512 * nb, 512 * nb + 512)
                pe.matmul(ps[:, 5 + k % 2, :], row, yg_hi[:, cs], start=True, stop=False)
                pe.matmul(ps[:, 5 + k % 2, :], row, yg_lo[:, cs], start=False, stop=True).then_inc(scat_done, 1)

            def gate_up(n, place, c4):
                pe.wait_ge(lo_ready, n + 1)
                r_hi, r_lo = (tile_views(w[:, place % SPL, :], "gu") for w in (w_hi, w_lo))
                for c in range(4):
                    ins = split3(ps[:, 4, :], xg_hi[:, 4 * c4 + c, :], xg_lo[:, 4 * c4 + c, :], r_hi[:, :, c, :],
                                 r_lo[:, :, c, :], start=(c4 == 0 and c == 0), stop=(c4 == 3 and c == 3))
                used(ins)

            def hidden_T(q, e):
                pe.wait_ge(h_ready, EPG * q + e + 1)
                for f in range(2):
                    ins = pe.transpose(ps[:, 7, P * f:P * f + P], hval[:, f::2], ident[:, :])
                ins.then_inc(hT_done, 1)

            def down(n, place, half, start=False, ks=range(2)):
                pe.wait_ge(lo_ready, n + 1)
                r_hi, r_lo = (tile_views(w[:, place % SPL, :], "down") for w in (w_hi, w_lo))
                for k in ks:
                    for f in range(2):
                        ins = split3(ps[:, 2 * half + k, :], hT_hi[:, f, :], hT_lo[:, f, :],
                                     r_hi[:, f, 512 * k:512 * k + 512], r_lo[:, f, 512 * k:512 * k + 512],
                                     start=start and f == 0, stop=False)
                if 1 in ks:
                    used(ins)

            def second_expert(q, n0):
                gate_up(n0 + 6, 6, 2)
                gate_up(n0 + 7, 7, 3)
                pe.wait_ge(hTlo_ready, EPG * q + 1)
                pe.wait_ge(rank_kept, 1)
                down(n0 + 8, 8, 0, start=True)
                down(n0 + 9, 9, 1, start=True)
                hidden_T(q, 1)

            def first_expert(q):
                n0 = first_of(q)
                pe.wait_ge(sel_ready, q + 1)
                gather(q, 0)
                for c4 in range(4):
                    if c4 < 3:
                        gather(q, c4 + 1)
                    pe.wait_ge(xglo_ready, 4 * q + c4 + 1)
                    gate_up(n0 + c4, c4, c4)
                pe.wait_ge(cmb_ready, 1)
                take_shares(q)
                hidden_T(q, 0)
                gate_up(n0 + 4, 4, 0)
                gate_up(n0 + 5, 5, 1)
                transpose_sel()
                second_expert(q, n0)

            def other_experts(q, into_next):
                n0 = first_of(q)
                with pe.Fori(2, EPG - 1) as j:
                    base = n0 + 6 * j - 2
                    for c4 in range(4):
                        gate_up(base + c4, 4 + c4, c4)
                        pe.wait_ge(hTlo_ready, EPG * q + j)
                    for half in range(2):
                        down(base + 4 + half, 2 + half, half)
                    hidden_T(q, j)
                for c4 in range(4):
                    gate_up(n0 + 40 + c4, 4 + c4, c4)
                    pe.wait_ge(hTlo_ready, EPG * q + EPG - 1)
                if into_next:
                    pe.wait_ge(selT_ready, q + 1)
                    take_shares(q + 1)
                    gather(q + 1, 0)
                    gather(q + 1, 1)
                down(n0 + 44, 2, 0)
                if into_next:
                    gather(q + 1, 2)
                down(n0 + 45, 3, 1)
                if into_next:
                    pe.wait_ge(share_ready, q + 2)
                hidden_T(q, EPG - 1)
                if into_next:
                    gather(q + 1, 3)
                pe.wait_ge(hTlo_ready, EPG * q + EPG)
                down(n0 + 46, 4, 0)
                pe.wait_ge(selT_ready, q + 1)
                if into_next:
                    down(n0 + 47, 5, 1)
                    pe.wait_ge(xglo_ready, 4 * q + 8)
                    gate_up(n0 + 48, 0, 0)
                    gate_up(n0 + 49, 1, 1)
                    gate_up(n0 + 50, 2, 2)
                    scatter(q, 0)
                    scatter(q, 1)
                    gate_up(n0 + 51, 3, 3)
                    for k in range(2, 6):
                        scatter(q, k)
                    hidden_T(q + 1, 0)
                    gate_up(n0 + 52, 4, 0)
                    scatter(q, 6)
                    scatter(q, 7)
                    gate_up(n0 + 53, 5, 1)
                    pe.wait_ge(scat_added, 8 * q + 7)
                    transpose_sel()
                    second_expert(q + 1, n0 + PER_GRP)
                else:
                    down(n0 + 47, 5, 1, ks=(0,))
                    for k in range(4):
                        scatter(q, k)
                    down(n0 + 47, 5, 1, ks=(1,))
                    for k in range(4, 8):
                        scatter(q, k)
                    pe.wait_ge(scat_added, 8 * q + 8)

            pe.wait_ge(hn_ready, 2)
            first_expert(0)
            with pe.Fori(0, NGRP - 1) as q:
                other_experts(q, True)
            other_experts(NGRP - 1, False)
            overflow = pe.value_load(flags[0:1, 0:1], min_val=0, max_val=1)
            with pe.If(overflow > 0):
                first_expert(NGRP)
                other_experts(NGRP, False)


_PARAMS = ["norm1_w", "w_in", "pool_w", "pool_scale", "conv_w", "cmp_pe_k", "cmp_w1_k", "cmp_w2_k", "cmp_pe_v",
           "cmp_w1_v", "cmp_w2_v", "q_norm_w", "k_norm_w", "w_out", "norm2_w", "router_grp_w", "router_grp_b",
           "router_exp_w", "router_exp_b", "exp_w_gate", "exp_w_up", "exp_w_down"]


def build(nc, arrays):
    args = {n: nc.dram_tensor(f"in_{n}", a.shape, F32, kind="ExternalInput").ap() for n, a in arrays.items()}
    out = nc.dram_tensor("out_0", (S, D), F32, kind="ExternalOutput").ap()
    layer_kernel(nc, *args.values(), out)


def kernel(**inputs):
    import concourse.bacc as bacc
    from concourse.bass_utils import run_bass_kernel_spmd

    nc = bacc.Bacc("TRN2", target_bir_lowering=False, num_devices=1, dynamic_dma_scratch_size=1024)
    arrays = {"x": np.ascontiguousarray(inputs["x"])[0]}
    for name in _PARAMS:
        arrays[name] = np.ascontiguousarray(inputs[name])[0]
    arrays["pool_edge"] = np.array([[1.0 / min(t + 1, w) for t in range(16)] for w in WINDOWS], np.float32)
    build(nc, arrays)
    r = run_bass_kernel_spmd(nc, [{f"in_{n}": a for n, a in arrays.items()}], core_ids=[0])
    return r.results[0]["out_0"][None]
```
